# Optimizing a Trainium2 kernel written in Bass

```python
import numpy as np
import jax, jax.numpy as jnp
from jax import lax

D_MODEL = 1024
BATCH = 1
SEQ = 1024
DEPTH = 2

HEAD_DIM = 64
N_HEADS = D_MODEL // HEAD_DIM
MIX_WIDTH = N_HEADS * HEAD_DIM
ROT_DIM = HEAD_DIM // 4
ROPE_THETA = 500000.0
BLK = 128
NORM_EPS = 1e-6
MASK_VALUE = -1e30
N_MIXERS = 4
SCALE = HEAD_DIM ** -0.5

SWA_KV = 4
SWA_WINDOW = 128
DIL_KV = 4
DIL_PATTERNS = ((128, 1), (512, 4), (2048, 16))
FOX_HEADS = N_HEADS
NSA_KV = 2
CMP_LEN = 32
CMP_STRIDE = 16
CMP_HIDDEN = 256
SEL_LEN = 64
SEL_TOPK = 8
NSA_WINDOW = 256
FORCED_SCORE = 1e4

kernel_name = "interleaved_hybrid_swa_dilated_fox_nsa"

def rms_norm(x, g):
    xf = x.astype(jnp.float32)
    y = xf * lax.rsqrt(jnp.mean(xf * xf, axis=-1, keepdims=True) + NORM_EPS)
    return (y * g.astype(jnp.float32)).astype(x.dtype)

def partial_rope(x, pos):
    half = ROT_DIM // 2
    inv = jnp.power(ROPE_THETA, -jnp.arange(half, dtype=jnp.float32) / half)
    ang = pos.astype(jnp.float32)[..., None] * inv
    cos = jnp.cos(ang)[:, :, None, :]
    sin = jnp.sin(ang)[:, :, None, :]
    xf = x.astype(jnp.float32)
    x1, x2, rest = xf[..., :half], xf[..., half:ROT_DIM], xf[..., ROT_DIM:]
    out = jnp.concatenate([x1 * cos - x2 * sin, x2 * cos + x1 * sin, rest], axis=-1)
    return out.astype(x.dtype)

def split_cols(t, sizes):
    return jnp.split(t, [int(c) for c in np.cumsum(sizes)[:-1]], axis=-1)

def masked_softmax(s, mask, axis):
    s = jnp.where(mask, s, MASK_VALUE)
    m = jnp.max(s, axis=axis, keepdims=True)
    p = jnp.where(mask, jnp.exp(s - m), 0.0)
    den = jnp.sum(p, axis=axis, keepdims=True)
    return p / jnp.maximum(den, 1e-30)

def banded_attention(q, k, v, max_dist, sink=None):
    B, S, H, Dh = q.shape
    G = k.shape[2]
    R = H // G
    nb = S // BLK
    n_prev = -(-max_dist // BLK)
    pad = n_prev * BLK
    kp = jnp.pad(k, ((0, 0), (pad, 0), (0, 0), (0, 0))).reshape(B, nb + n_prev, BLK, G, Dh)
    vp = jnp.pad(v, ((0, 0), (pad, 0), (0, 0), (0, 0))).reshape(B, nb + n_prev, BLK, G, Dh)
    kb = jnp.concatenate([kp[:, j:j + nb] for j in range(n_prev + 1)], axis=2)
    vb = jnp.concatenate([vp[:, j:j + nb] for j in range(n_prev + 1)], axis=2)
    qb = q.reshape(B, nb, BLK, G, R, Dh)
    s = jnp.einsum('bnqgrd,bnkgd->bngrqk', qb, kb).astype(jnp.float32) * SCALE
    qi = jnp.arange(BLK)
    ki = jnp.arange((n_prev + 1) * BLK) - pad
    dist = qi[:, None] - ki[None, :]
    band = (dist >= 0) & (dist <= max_dist)
    start = jnp.arange(nb) * BLK
    mask = band[None] & ((start[:, None] + ki[None, :]) >= 0)[:, None, :]
    mask = mask[None, :, None, None]
    s = jnp.where(mask, s, MASK_VALUE)
    m = jnp.max(s, axis=-1, keepdims=True)
    if sink is not None:
        sk = sink.astype(jnp.float32).reshape(1, 1, G, R, 1, 1)
        m = jnp.maximum(m, sk)
    p = jnp.where(mask, jnp.exp(s - m), 0.0)
    den = jnp.sum(p, axis=-1, keepdims=True)
    if sink is not None:
        den = den + jnp.exp(sk - m)
    o = jnp.einsum('bngrqk,bnkgd->bnqgrd', (p / den).astype(v.dtype), vb).reshape(B, S, H, Dh)
    lse = (m + jnp.log(den))[..., 0].transpose(0, 1, 4, 2, 3).reshape(B, S, H)
    return o, lse

def swa_sink_mixer(h, pos, w_in, sinks):
    B, S, _ = h.shape
    q, k, v, gate = split_cols(h @ w_in, [MIX_WIDTH, SWA_KV * HEAD_DIM, SWA_KV * HEAD_DIM, MIX_WIDTH])
    q = partial_rope(q.reshape(B, S, N_HEADS, HEAD_DIM), pos)
    k = partial_rope(k.reshape(B, S, SWA_KV, HEAD_DIM), pos)
    v = v.reshape(B, S, SWA_KV, HEAD_DIM)
    o, _ = banded_attention(q, k, v, SWA_WINDOW - 1, sinks)
    return o.reshape(B, S, MIX_WIDTH) * jax.nn.silu(gate)

def dilated_attention(q, k, v, window, dil):
    B, S, H, Dh = q.shape
    seg = dil * BLK
    Sp = -(-S // seg) * seg
    L = Sp // dil

    def to_sub(t):
        n = t.shape[2]
        t = jnp.pad(t, ((0, 0), (0, Sp - S), (0, 0), (0, 0)))
        t = t.reshape(B, L, dil, n, Dh).transpose(0, 2, 1, 3, 4)
        return t.reshape(B * dil, L, n, Dh)

    o, lse = banded_attention(to_sub(q), to_sub(k), to_sub(v), window // dil)
    o = o.reshape(B, dil, L, H, Dh).transpose(0, 2, 1, 3, 4).reshape(B, Sp, H, Dh)[:, :S]
    lse = lse.reshape(B, dil, L, H).transpose(0, 2, 1, 3).reshape(B, Sp, H)[:, :S]
    return o, lse

def dilated_mixer(h, pos, w_in):
    B, S, _ = h.shape
    per_group = [MIX_WIDTH, DIL_KV * HEAD_DIM, DIL_KV * HEAD_DIM]
    cols = split_cols(h @ w_in, per_group * len(DIL_PATTERNS) + [MIX_WIDTH])
    gate = cols[-1]
    outs, lses = [], []
    for gi, (window, dil) in enumerate(DIL_PATTERNS):
        q, k, v = cols[3 * gi:3 * gi + 3]
        q = partial_rope(q.reshape(B, S, N_HEADS, HEAD_DIM), pos)
        k = partial_rope(k.reshape(B, S, DIL_KV, HEAD_DIM), pos)
        v = v.reshape(B, S, DIL_KV, HEAD_DIM)
        o, lse = dilated_attention(q, k, v, window, dil)
        outs.append(o)
        lses.append(lse)
    w = jax.nn.softmax(jnp.stack(lses, axis=0), axis=0)
    o = jnp.sum(w[..., None].astype(outs[0].dtype) * jnp.stack(outs, axis=0), axis=0)
    return o.reshape(B, S, MIX_WIDTH) * jax.nn.silu(gate)

def fox_mixer(h, w_in, b_f):
    B, S, _ = h.shape
    H = FOX_HEADS
    q, k, v, f_logit, gate = split_cols(h @ w_in, [MIX_WIDTH, MIX_WIDTH, MIX_WIDTH, H, MIX_WIDTH])
    q = q.reshape(B, S, H, HEAD_DIM)
    k = k.reshape(B, S, H, HEAD_DIM)
    v = v.reshape(B, S, H, HEAD_DIM)
    logf = jax.nn.log_sigmoid(f_logit.astype(jnp.float32) + b_f.astype(jnp.float32))
    c = jnp.cumsum(logf, axis=1)
    nb = S // BLK
    qb = q.reshape(B, nb, BLK, H, HEAD_DIM).transpose(1, 0, 2, 3, 4)
    cb = c.reshape(B, nb, BLK, H).transpose(1, 0, 2, 3)
    ck = c.transpose(0, 2, 1)[:, :, None, :]
    kpos = jnp.arange(S)

    def block(args):
        qn, cn, n = args
        s = jnp.einsum('bqhd,bkhd->bhqk', qn, k).astype(jnp.float32) * SCALE
        s = s + cn.transpose(0, 2, 1)[..., None] - ck
        t = n * BLK + jnp.arange(BLK)
        p = masked_softmax(s, kpos[None, :] <= t[:, None], -1)
        return jnp.einsum('bhqk,bkhd->bqhd', p.astype(v.dtype), v)

    o = lax.map(block, (qb, cb, jnp.arange(nb)))
    o = o.transpose(1, 0, 2, 3, 4).reshape(B, S, MIX_WIDTH)
    return o * jax.nn.silu(gate)

def compress_blocks(t, pe, w1, w2):
    B, S, G, Dh = t.shape
    ns = S // CMP_STRIDE
    tb = t.reshape(B, ns, CMP_STRIDE, G, Dh)
    win = jnp.concatenate([tb[:, :-1], tb[:, 1:]], axis=2)
    win = win + pe[None, None, :, None, :].astype(t.dtype)
    flat = win.transpose(0, 1, 3, 2, 4).reshape(B, ns - 1, G, CMP_LEN * Dh)
    return jax.nn.gelu(flat @ w1) @ w2

def selection_overlap(n_cmp, n_sel):
    cs = np.arange(n_cmp) * CMP_STRIDE
    js = np.arange(n_sel) * SEL_LEN
    ov = np.minimum(cs[:, None] + CMP_LEN, js[None, :] + SEL_LEN) - np.maximum(cs[:, None], js[None, :])
    return (np.clip(ov, 0, None) / CMP_LEN).astype(np.float32)

def nsa_mixer(h, pos, w_in, cmp_pe_k, cmp_w1_k, cmp_w2_k, cmp_pe_v, cmp_w1_v, cmp_w2_v):
    B, S, _ = h.shape
    H, G = N_HEADS, NSA_KV
    R = H // G
    kvw = G * HEAD_DIM
    q, kc, vc, ks, vs, kw, vw, g_logit, gate = split_cols(
        h @ w_in, [MIX_WIDTH, kvw, kvw, kvw, kvw, kvw, kvw, 3 * H, MIX_WIDTH])
    q = partial_rope(q.reshape(B, S, H, HEAD_DIM), pos)
    k_cmp = compress_blocks(kc.reshape(B, S, G, HEAD_DIM), cmp_pe_k, cmp_w1_k, cmp_w2_k)
    v_cmp = compress_blocks(vc.reshape(B, S, G, HEAD_DIM), cmp_pe_v, cmp_w1_v, cmp_w2_v)
    n_cmp = k_cmp.shape[1]
    cmp_end = np.arange(n_cmp) * CMP_STRIDE + CMP_LEN - 1
    k_cmp = partial_rope(k_cmp, pos[:, cmp_end])
    cmp_end_j = jnp.asarray(cmp_end)
    n_sel = S // SEL_LEN
    k_sel_n = min(SEL_TOPK, n_sel)
    ks = partial_rope(ks.reshape(B, S, G, HEAD_DIM), pos)
    ks = ks.reshape(B, n_sel, SEL_LEN, G, HEAD_DIM).transpose(0, 3, 1, 2, 4)
    vs = vs.reshape(B, n_sel, SEL_LEN, G, HEAD_DIM).transpose(0, 3, 1, 2, 4)
    overlap = jnp.asarray(selection_overlap(n_cmp, n_sel))
    nb = S // BLK
    qb = q.reshape(B, nb, BLK, G, R, HEAD_DIM).transpose(1, 0, 2, 3, 4, 5)
    bi = jnp.arange(B)[:, None, None, None]
    gi = jnp.arange(G)[None, :, None, None]
    jsel = jnp.arange(n_sel)

    def block(args):
        qn, n = args
        t = n * BLK + jnp.arange(BLK)
        s = jnp.einsum('bqgrd,bcgd->bgrqc', qn, k_cmp).astype(jnp.float32) * SCALE
        p_cmp = masked_softmax(s, cmp_end_j[None, :] <= t[:, None], -1)
        o_cmp = jnp.einsum('bgrqc,bcgd->bqgrd', p_cmp.astype(v_cmp.dtype), v_cmp)
        imp = jnp.einsum('bgrqc,cj->bgqj', p_cmp, overlap)
        cur = t // SEL_LEN
        forced = (jsel[None, :] == 0) | (jsel[None, :] == cur[:, None])
        causal = jsel[None, :] <= cur[:, None]
        score = jnp.where(causal, jnp.where(forced, FORCED_SCORE, imp), MASK_VALUE)
        vals, idx = lax.top_k(score, k_sel_n)
        valid = vals > 0.5 * MASK_VALUE
        kg = ks[bi, gi, idx]
        vg = vs[bi, gi, idx]
        tok = idx[..., None] * SEL_LEN + jnp.arange(SEL_LEN)
        smask = valid[..., None] & (tok <= t[None, None, :, None, None])
        s2 = jnp.einsum('bqgrd,bgqkld->bgqrkl', qn, kg).astype(jnp.float32) * SCALE
        p_slc = masked_softmax(s2, smask[:, :, :, None], (-2, -1))
        o_slc = jnp.einsum('bgqrkl,bgqkld->bqgrd', p_slc.astype(vg.dtype), vg)
        return o_cmp, o_slc

    o_cmp, o_slc = lax.map(block, (qb, jnp.arange(nb)))
    o_cmp = o_cmp.transpose(1, 0, 2, 3, 4, 5).reshape(B, S, H, HEAD_DIM)
    o_slc = o_slc.transpose(1, 0, 2, 3, 4, 5).reshape(B, S, H, HEAD_DIM)
    kw = partial_rope(kw.reshape(B, S, G, HEAD_DIM), pos)
    vw = vw.reshape(B, S, G, HEAD_DIM)
    o_win, _ = banded_attention(q, kw, vw, NSA_WINDOW - 1)
    g = jax.nn.sigmoid(g_logit.astype(jnp.float32)).reshape(B, S, H, 3, 1).astype(h.dtype)
    o = g[:, :, :, 0] * o_cmp + g[:, :, :, 1] * o_slc + g[:, :, :, 2] * o_win
    return o.reshape(B, S, MIX_WIDTH) * jax.nn.silu(gate)

def setup_inputs(seed: int = 0) -> dict:
    key = jax.random.key(seed)
    ks = jax.random.split(key, 24)
    f32 = jnp.float32

    def w(k, shape):
        return jax.random.normal(k, shape, f32) * shape[0] ** -0.5

    def gain(k):
        return 1.0 + 0.05 * jax.random.normal(k, (D_MODEL,), f32)

    kvw = NSA_KV * HEAD_DIM
    in_a = 2 * MIX_WIDTH + 2 * SWA_KV * HEAD_DIM
    in_b = len(DIL_PATTERNS) * (MIX_WIDTH + 2 * DIL_KV * HEAD_DIM) + MIX_WIDTH
    in_c = 4 * MIX_WIDTH + FOX_HEADS
    in_d = 2 * MIX_WIDTH + 6 * kvw + 3 * N_HEADS
    return {
        "x": jax.random.normal(ks[0], (BATCH, SEQ, D_MODEL), f32),
        "positions": (jnp.arange(SEQ, dtype=jnp.int32)[None, :]
                      + jax.random.randint(ks[1], (BATCH, 1), 0, 4096, dtype=jnp.int32)),
        "norm_0": gain(ks[2]),
        "w_in_0": w(ks[3], (D_MODEL, in_a)),
        "sinks_0": 0.5 * jax.random.normal(ks[4], (N_HEADS,), f32),
        "w_out_0": w(ks[5], (MIX_WIDTH, D_MODEL)),
        "norm_1": gain(ks[6]),
        "w_in_1": w(ks[7], (D_MODEL, in_b)),
        "w_out_1": w(ks[8], (MIX_WIDTH, D_MODEL)),
        "norm_2": gain(ks[9]),
        "w_in_2": w(ks[10], (D_MODEL, in_c)),
        "b_f_2": 3.0 + 0.5 * jax.random.normal(ks[11], (FOX_HEADS,), f32),
        "w_out_2": w(ks[12], (MIX_WIDTH, D_MODEL)),
        "norm_3": gain(ks[13]),
        "w_in_3": w(ks[14], (D_MODEL, in_d)),
        "cmp_pe_k_3": 0.02 * jax.random.normal(ks[15], (CMP_LEN, HEAD_DIM), f32),
        "cmp_w1_k_3": w(ks[16], (CMP_LEN * HEAD_DIM, CMP_HIDDEN)),
        "cmp_w2_k_3": w(ks[17], (CMP_HIDDEN, HEAD_DIM)),
        "cmp_pe_v_3": 0.02 * jax.random.normal(ks[18], (CMP_LEN, HEAD_DIM), f32),
        "cmp_w1_v_3": w(ks[19], (CMP_LEN * HEAD_DIM, CMP_HIDDEN)),
        "cmp_w2_v_3": w(ks[20], (CMP_HIDDEN, HEAD_DIM)),
        "w_out_3": w(ks[21], (MIX_WIDTH, D_MODEL)),
        "final_norm": gain(ks[22]),
    }

def reference(x, positions, norm_0, w_in_0, sinks_0, w_out_0, norm_1, w_in_1, w_out_1,
              norm_2, w_in_2, b_f_2, w_out_2, norm_3, w_in_3, cmp_pe_k_3, cmp_w1_k_3,
              cmp_w2_k_3, cmp_pe_v_3, cmp_w1_v_3, cmp_w2_v_3, w_out_3, final_norm):
    layers = [
        (norm_0, lambda h: swa_sink_mixer(h, positions, w_in_0, sinks_0), w_out_0),
        (norm_1, lambda h: dilated_mixer(h, positions, w_in_1), w_out_1),
        (norm_2, lambda h: fox_mixer(h, w_in_2, b_f_2), w_out_2),
        (norm_3, lambda h: nsa_mixer(h, positions, w_in_3, cmp_pe_k_3, cmp_w1_k_3, cmp_w2_k_3,
                                     cmp_pe_v_3, cmp_w1_v_3, cmp_w2_v_3), w_out_3),
    ]
    for i in range(DEPTH):
        norm, mixer, w_out = layers[i % N_MIXERS]
        x = x + mixer(rms_norm(x, norm)) @ w_out
    return rms_norm(x, final_norm)


_drawn_inputs = setup_inputs


def setup_inputs(seed=0):
    import zlib

    import numpy as np

    out = dict(_drawn_inputs(seed))
    spreads = {}
    factors = {'norm_0': 5.771, 'sinks_0': 8.0, 'norm_1': 7.427}
    for name, (base, spread) in spreads.items():
        noise = np.random.default_rng([zlib.crc32(name.encode()), seed]).standard_normal(out[name].shape)
        drawn = base * np.exp(spread * noise) if base else spread * noise
        out[name] = __import__('jax').numpy.asarray(drawn.astype(out[name].dtype))
    for name, factor in factors.items():
        out[name] = (out[name] * factor).astype(out[name].dtype)
    return out
```

```python
from contextlib import ExitStack

import numpy as np
import concourse.bass as bass
from concourse import mybir

F32 = mybir.dt.float32
F32R = mybir.dt.float32r
I32 = mybir.dt.int32
ALU = mybir.AluOpType
ACT = mybir.ActivationFunctionType

P = 128
S = 1024
D = 1024
KT = D // P
NB = S // P
HD = 64
HALF_ROT = 8
ROT = 2 * HALF_ROT
H = 16
GROUPS = 4
R = H // GROUPS
SCALE = HD ** -0.5
EPS = 1e-6
THETA = 500000.0
MASKED = -1e30
QKV = R * HD + 2 * HD
KV = GROUPS * HD
PER = D + 2 * KV
OUT_COLS = 256
OUT_JOBS = D // OUT_COLS
UNITS = 2 * NB
BIG = 3.0e38
PROBS = 3



class Step:
    def __init__(self, t, layer, g, p):
        self.t, self.layer, self.g, self.p = t, layer, g, p
        self.last = (g == GROUPS - 1) and (layer == 0 or p == 2)
        self.first = g == 0 and p == 0
        self.ends_group = layer == 0 or p == 2

    def has_prev(self, n):
        return (n > 0) if self.p == 0 else (n % 2 == 1) if self.p == 1 else False


STEPS = [Step(g, 0, g, 0) for g in range(GROUPS)]
STEPS += [Step(GROUPS + 3 * g + p, 1, g, p) for g in range(GROUPS) for p in range(3)]
LAYER_STEPS = [[s for s in STEPS if s.layer == layer] for layer in (0, 1)]

JOBS = []
SLOT_SPLIT = {}
SLOT_PIECES = {}
SLOT_RAW = {}
for _layer in (0, 1):
    _steps = LAYER_STEPS[_layer]
    JOBS.append(("qkv", _steps[0].t))
    for _s in _steps:
        _t = _s.t
        _slots = []
        if not _s.last:
            JOBS.append(("qkv", _t + 1))
            _slots.append((JOBS[-1], 0, [4, 4, 5, 5, 6, 6, 7, 7] if _s.ends_group else [4, 5, 7, 8, 10, 11, 13, 14]))
        if _s.ends_group:
            JOBS.append(("gate", _layer, _s.g))
            if _s.last:
                _slots.append((JOBS[-1], 0, [10, 11, 12, 13] if _layer == 0 else [4, 7, 10, 13]))
            else:
                _slots.append((JOBS[-1], 8, [12, 13, 14, 15]))
        for _job, _at, _pieces in _slots:
            for _q in range(4):
                SLOT_SPLIT[_t, _at + _q] = (_job, _q)
            SLOT_RAW[_t, _at + 4] = _job
            for _k, _slot in enumerate(_pieces):
                SLOT_PIECES.setdefault((_t, _slot), []).append(_job + (_k,))
    for _c in range(OUT_JOBS):
        JOBS.append(("out", _layer, _c))
JOB = {job: n for n, job in enumerate(JOBS)}


def columns(job):
    return {"qkv": QKV, "gate": R * HD, "out": OUT_COLS}[job[0]]


def packed_index(job):
    return job[1] if job[0] == "qkv" else 4 * job[1] + job[2]


def second_buffer(job):
    return job[0] == "out" and job[2] % 2 == 0


def previous_in_buffer(job):
    n = JOB[job] - 1
    while n >= 0 and second_buffer(JOBS[n]) != second_buffer(job):
        n -= 1
    return n


FILLS_BEFORE = {13: ("K", 0), 14: ("Q0", 0), 15: ("Q1", 0)}
FILLS_WITHIN = {1: ("K", 1), 2: ("Q0", 1), 3: ("Q1", 1)}
LATE_C = 5
MIX_AT = {0: 8, 1: 9}


class Ring:

    def __init__(self):
        self.uses, self.at = [], {}

    def add(self, key, by):
        self.at[key] = len(self.uses)
        self.uses.append(by)

    def bank(self, key):
        return self.at[key] % 2

    def filled(self, key):
        return self.at[key] + 1

    def emptied(self, key, engine):
        return sum(engine in by for by in self.uses[: self.at[key] + 1])

    def free(self, key):
        k = self.at[key] - 2
        if k < 0:
            return []
        return [(e, sum(e in by for by in self.uses[: k + 1])) for e in "av" if any(e in by for by in self.uses[: k + 1])]


def unit_before(s, u, back):
    u -= back
    if u >= 0:
        return s, u
    return (None, None) if s.first else (STEPS[s.t - 1], u + UNITS)


PIECE = Ring()
TURN = Ring()
for _layer in (0, 1):
    _first = LAYER_STEPS[_layer][0]
    for _kt in range(KT):
        PIECE.add(("norm", _layer, _kt, 0), "av")
    for _k in range(NB):
        PIECE.add(("qkv", _first.t, _k), "av"[_k % 2])
        if _k < 4:
            for _kt in (2 * _k, 2 * _k + 1):
                PIECE.add(("norm", _layer, _kt, 1), "av")
    for _what, _half in FILLS_BEFORE.values():
        TURN.add((_first.t, _what, _half), "av")
    for _s in LAYER_STEPS[_layer]:
        for _slot in range(UNITS):
            for _n, _piece in enumerate(SLOT_PIECES.get((_s.t, _slot), [])):
                PIECE.add(_piece, "av"[_piece[-1] % 2])
            _b, _u = unit_before(_s, _slot, 1)
            if _b:
                TURN.add((_b.t, _u), "av"[_u % 2])
            if _slot in FILLS_WITHIN:
                TURN.add((_s.t,) + FILLS_WITHIN[_slot], "av")
            if _slot in FILLS_BEFORE and not _s.last:
                TURN.add((_s.t + 1,) + FILLS_BEFORE[_slot], "av")
            if _slot == LATE_C and not _s.first and STEPS[_s.t - 1].ends_group:
                TURN.add(("C", _s.t - 1), "v")
    TURN.add((_s.t, UNITS - 1), "av"[(UNITS - 1) % 2])
    TURN.add(("C", _s.t), "v")
    for _c in range(OUT_JOBS):
        for _k in range(NB):
            PIECE.add(("out", _layer, _c, _k), "v")


def patterned(view, p, half):
    if p == 0:
        return view[:, half * 512:(half + 1) * 512].rearrange("a (b c) -> a b c", b=1)
    f = 4 if p == 1 else 8
    return view.rearrange("a (i f) -> a f i", f=f)[:, half * (f // 2):(half + 1) * (f // 2), :]


def block_positions(view, p, n):
    if p == 0:
        return view[:, n * P:(n + 1) * P]
    if p == 1:
        start = n // 2 + 512 * (n % 2)
        return view[:, start:start + 4 * (P - 1) + 1:4]
    return view[:, n:n + 8 * (P - 1) + 1:8]


def trunk(nc, x, positions, gains, sinks_0, final_norm, w_qkv, w_gate, w_out, out):
    ctx = ExitStack()
    with ctx:
        def sb(name, shape, dt=F32):
            return ctx.enter_context(nc.sbuf_tensor(name, shape, dt))

        def sem(name):
            return ctx.enter_context(nc.semaphore(name))

        def bank(name):
            return ctx.enter_context(nc.psum_tensor(name, [P, 512], F32))

        ht = [sb("ht_hi", [P, KT, S], F32R), sb("ht_lo", [P, KT, S], F32R)]
        w_raw = sb("w_raw", [P, KT, QKV])
        w_split = [sb("w_hi", [P, KT, QKV], F32R), sb("w_lo", [P, KT, QKV], F32R)]
        qk = sb("qk", [P, NB, R * HD + 2 * HD])
        v = sb("v", [P, 2, NB, HD])
        qs = sb("qs", [P, R, S], F32R)
        ks = sb("ks", [P, 2, S], F32R)
        probs = sb("probs", [P, PROBS, 2, 2, P])
        probs_t = sb("probs_t", [P, 2, 4, P])
        xr = sb("xr", [P, NB, D])
        ot = [xr[:, 2 * i:2 * i + 2, :] for i in range(4)]
        gate = sb("gate", [P, 2, S])
        coef = sb("coef", [P, 2, S])
        masks = sb("masks", [P, 4, P])
        ident = sb("ident", [P, P])
        stat = sb("stat", [P, 2, NB, 2 * R])
        nat = sb("nat", [P, 3, NB, 2 * R])
        comb = sb("comb", [P, 2, 3, NB, R])
        comb_small = sb("comb_small", [P, 2, NB, R])
        coef_rows = sb("coef_rows", [3 * NB * R, P])
        mx = sb("mx", [P, 2, 2])
        sink = sb("sink", [P, H])
        neg_sink = sb("neg_sink", [P, H])
        no_sink = sb("no_sink", [P, 2])
        pos_i = sb("pos_i", [P, 3, NB], I32)
        pos_f = sb("pos_f", [P, 3, NB])
        rope_w = gate[:, 0, 0:9 * NB * HALF_ROT].rearrange("p (a b) -> p a b", a=3)
        cosines = sb("cosines", [P, 3, NB, ROT])
        sines = sb("sines", [P, 3, NB, ROT])
        rot = sb("rot", [P, 2, 6, ROT])
        gain = sb("gain", [P, 2, KT])
        ssq = sb("ssq", [P, 4, NB])
        sums = sb("sums", [P, NB])

        s_bank = [bank(f"s_bank{i}") for i in range(2)]
        t_bank = [bank(f"t_bank{i}") for i in range(2)]
        o_bank = [bank(f"o_bank{i}") for i in range(2)]
        j_bank = [bank(f"j_bank{i}") for i in range(2)]

        def dram(name, shape):
            return nc.dram_tensor(name, shape, F32).ap()

        mix_dram = dram("mix_dram", [2, D, S])
        x1_dram = dram("x1_dram", [S, D])
        stat_dram = dram("stat_dram", [GROUPS * 3, S, 2 * R])
        coef_dram = dram("coef_dram", [2 * GROUPS, 3, NB, R, P])

        x2d = x.rearrange("a s d -> (a s) d")
        out2d = out.rearrange("a s d -> (a s) d")
        packed = {"qkv": w_qkv, "gate": w_gate, "out": w_out}
        w_out_hi = qs[:, 0:2, :].rearrange("p a (b c) -> p (a b) c", c=OUT_COLS)
        w_out_lo = qs[:, 2:4, :].rearrange("p a (b c) -> p (a b) c", c=OUT_COLS)
        res = [gate[:, :, :].rearrange("p a (b c) -> p (a b) c", c=OUT_COLS),
               coef[:, :, :].rearrange("p a (b c) -> p (a b) c", c=OUT_COLS)]
        mix_in = [qk[:, :, :].rearrange("p a b -> p (a b)")[:, i * S:(i + 1) * S] for i in range(3)]
        square_a = probs_t[:, :, :, :].rearrange("p a b c -> p (a b c)")
        square_v = probs[:, :, :, :, :].rearrange("p a b c d -> p (a b c d)")[:, 0:D]
        gain_row = qk[:, :, :].rearrange("p a b -> p (a b)")[:, 0:D]

        def weights(job, part):
            if second_buffer(job):
                return (w_out_hi, w_out_lo)[part]
            return w_split[part][:, :, 0:columns(job)]

        parity = gate[:, 1, 0:P].bitcast(I32)

        x_in = [sem(f"x_in{i}") for i in range(NB)]
        small_in = sem("small_in")
        raw_in = sem("raw_in")
        mix_back = [sem(f"mix_back{i}") for i in range(3)]
        res_in = [sem(f"res_in{i}") for i in range(2)]
        nat_in = sem("nat_in")
        coef_in = [sem(f"coef_in{i}") for i in range(2)]
        gain_in = sem("gain_in")
        stat_out = [sem(f"stat_out{i}") for i in range(2)]
        coef_out = sem("coef_out")
        mix_out = sem("mix_out")
        x1_out = sem("x1_out")
        final_out = sem("final_out")
        piece_full = sem("piece_full")
        turned = sem("turned")
        job_done = sem("job_done")
        scored = sem("scored")
        summed = sem("summed")
        piece_empty = {"a": sem("piece_empty_a"), "v": sem("piece_empty_v")}
        turn_empty = {"a": sem("turn_empty_a"), "v": sem("turn_empty_v")}
        masked = sem("masked")
        biased = sem("biased")
        exped = sem("exped")
        w_hi_done = sem("w_hi_done")
        w_lo_done = {"v": sem("w_lo_v"), "p": sem("w_lo_p")}
        ot_stored = sem("ot_stored")
        silued = sem("silued")
        den_v = sem("den_v")
        den_a = sem("den_a")
        mixed = sem("mixed")
        mix_hi = sem("mix_hi")
        mix_lo = sem("mix_lo")
        squared = {"a": sem("squared_a"), "v": sem("squared_v")}
        norm_v = sem("norm_v")
        norm_a = sem("norm_a")
        xn_done = sem("xn_done")
        rope_v = sem("rope_v")
        rope_a = sem("rope_a")
        tables = sem("tables")
        sink_neg = sem("sink_neg")
        mask_v = sem("mask_v")
        norm_r = sem("norm_r")
        rotated = sem("rotated")
        rot_link = sem("rot_link")
        consts = sem("consts")
        const_link = sem("const_link")

        block = ctx.enter_context(nc.Block())

        def wait_piece_emptied(eng, key, by="av"):
            for e in by:
                if e in PIECE.uses[PIECE.at[key]]:
                    eng.wait_ge(piece_empty[e], PIECE.emptied(key, e))

        def wait_turn_emptied(eng, key):
            for e in TURN.uses[TURN.at[key]]:
                eng.wait_ge(turn_empty[e], TURN.emptied(key, e))

        def links_per_group(layer):
            return 4 if layer == 0 else 7

        def links_before(t):
            return sum(links_per_group(s.layer) for s in STEPS[:t] if s.ends_group)

        def groups_before(t):
            return sum(s.ends_group for s in STEPS[:t])

        def mix_items(s):
            return [(r, p) for r in range(2) for p in range(1 if s.layer == 0 else 3)]

        def mix_links(s):
            return sum(1 + (p > 0) for _, p in mix_items(s)) + 2

        def mix_links_before(t):
            return sum(mix_links(s) for s in STEPS[:t] if s.ends_group)

        def coef_loads_before(t):
            return sum(len(mix_items(s)) for s in STEPS[:t] if s.ends_group)

        def out_region(s):
            return (s.t - s.p) % 4

        MIX_LOADS = 2 * (GROUPS - 1)

        def stat_stored(t):
            return 16 * sum(2 if s.p == 1 else 1 for s in STEPS[GROUPS:t + 1] if s.t % 2 == t % 2)

        def product_link(index):
            seen = 0
            for s in STEPS:
                if s.ends_group:
                    done = mix_links_before(s.t)
                    for k, (r, p) in enumerate(mix_items(s)):
                        done += 1
                        if seen == index:
                            return done
                        seen += 1
                        if p > 0:
                            done += 1
                        if k + 1 == len(mix_items(s)) or mix_items(s)[k + 1][0] != r:
                            done += 1
            raise ValueError(index)

        NORM_LINKS = 6
        ROPE_LINKS = 26

        def row_ready(k):
            def wait(eng, n):
                if k == 0:
                    eng.wait_ge(x_in[n], 16)
                else:
                    eng.wait_ge(piece_empty["v"], PIECE.emptied(("out", k - 1, OUT_JOBS - 1, n), "v"))
            return wait

        def guard_qkv(eng, key):
            _, t, k = key
            s = STEPS[t]
            if not s.first:
                eng.wait_ge(turned, TURN.filled((t - 1, "Q1", k // 4)))
            elif t > 0:
                eng.wait_ge(mix_lo, MIX_LOADS + 2)
                eng.wait_ge(mix_hi, MIX_LOADS + 2)
            if t >= 2:
                eng.wait_ge(summed, UNITS * (t - 1))

        def guard_gate(eng, key):
            _, layer, g, k = key
            t = [s.t for s in STEPS if s.layer == layer and s.g == g and s.ends_group][0]
            if t > 0 and g > 0:
                eng.wait_ge(mixed, mix_links_before(t))
            elif layer == 1:
                eng.wait_ge(piece_empty["v"], PIECE.emptied(("out", 0, OUT_JOBS - 1, NB - 1), "v"))

        def guard_fill(eng, t, what, half):
            s = STEPS[t]
            if not s.first:
                last = 8 + 4 * half + 4 if what == "K" else 8 * int(what[1]) + 4 * half + 4
                if what == "K":
                    last = 13 if half == 0 else UNITS
                eng.wait_ge(scored, UNITS * (t - 1) + last)
            elif t > 0:
                eng.wait_ge(job_done, JOB[("out", 0, OUT_JOBS - 1)] + 1)

        def store_turn(eng, copy, s, u):
            r, n = u // NB, u % NB
            i = UNITS * s.t + u
            key = (s.t, u)
            eng.wait_ge(turned, TURN.filled(key))
            if i >= 2:
                eng.wait_ge(summed, i - 1)
            src = t_bank[TURN.bank(key)][:, :].rearrange("p (j e q) -> p j e q", j=2, e=2)
            to = probs_t[:, i % 2, :, :].rearrange("p (j e) q -> p j e q", e=2)
            lo = 0 if s.has_prev(n) else 1
            return copy(to[:, :, lo:2, :], src[:, :, lo:2, :])

        @block.sync
        def _(sp):
            def raw(job):
                n = JOB[job]
                if n > 0:
                    sp.wait_ge(w_lo_done["v"], 2 * n)
                    sp.wait_ge(w_lo_done["p"], 2 * n)
                cols = columns(job)
                sp.dma_start(w_raw[:, :, 0:cols], packed[job[0]][packed_index(job)].rearrange("p (k c) -> p k c", k=KT)).then_inc(raw_in, 16)

            def stats_out(s):
                sp.wait_ge(exped, UNITS * (s.t + 1))
                n = s.t - GROUPS
                src = stat[:, s.t % 2, :, :]
                if s.p == 0:
                    sp.dma_start(stat_dram[n].rearrange("(n i) c -> i n c", n=NB), src).then_inc(stat_out[s.t % 2], 16)
                elif s.p == 1:
                    to = stat_dram[n].rearrange("(b i f) c -> i b f c", b=2, f=4)
                    for b in range(2):
                        sp.dma_start(to[:, b, :, :], src[:, b:NB:2, :]).then_inc(stat_out[s.t % 2], 16)
                else:
                    sp.dma_start(stat_dram[n].rearrange("(i n) c -> i n c", n=NB), src).then_inc(stat_out[s.t % 2], 16)

            def stats_in(s):
                for q in (s.t - 1, s.t):
                    sp.wait_ge(stat_out[q % 2], stat_stored(q))
                if s.g > 0:
                    sp.wait_ge(den_v, links_before(s.t))
                for p in range(3):
                    sp.dma_start(nat[:, p, :, :], stat_dram[3 * s.g + p].rearrange("(n i) c -> i n c", n=NB)).then_inc(nat_in, 16)

            def coef_store(s):
                n = groups_before(s.t)
                rows = (1 if s.layer == 0 else 3) * NB * R
                sp.wait_ge(turn_empty["v"], TURN.emptied(("C", s.t), "v"))
                to = coef_dram[n].rearrange("p n h i -> (p n h) i")
                sp.dma_start(to[0:rows, :], coef_rows[0:rows, :]).then_inc(coef_out, 16)

            def coef_load(s, k):
                n = groups_before(s.t)
                r, p = mix_items(s)[k]
                index = coef_loads_before(s.t) + k
                buf = index % 2
                sp.wait_ge(coef_out, 16 * (n + 1))
                if index >= 2:
                    sp.wait_ge(mixed, product_link(index - 2))
                for j in range(2):
                    src = coef_dram[n, p, :, 2 * r + j, :]
                    src = src.rearrange("(o n) i -> o n i", o=1).broadcast_to([HD, NB, P])
                    sp.dma_start(coef[64 * j:64 * j + 64, buf, :].rearrange("p (n i) -> p n i", n=NB), src).then_inc(coef_in[buf], 16)

            def mix_store(s):
                sp.wait_ge(mixed, mix_links_before(s.t) + mix_links(s))
                for r in range(2):
                    row = (2 * s.g + r) * P
                    sp.dma_start(mix_dram[s.layer, row:row + P, :], ot[out_region(s)][:, r, :]).then_inc(mix_out, 16)

            def mix_load(layer, k):
                last = LAYER_STEPS[layer][-1]
                n = layer * MIX_LOADS + k
                sp.wait_ge(mix_out, 16 * 2 * (GROUPS - 1) * (layer + 1))
                if k < 3:
                    sp.wait_ge(turned, TURN.filled((last.t, "Q1", 1)))
                else:
                    sp.wait_ge(mix_lo, layer * (MIX_LOADS + 2) + k - 2)
                sp.dma_start(mix_in[k % 3], mix_dram[layer, k * P:(k + 1) * P, :]).then_inc(mix_back[n % 3], 16)

            def res_load(layer, c):
                if c < 2:
                    sp.wait_ge(mixed, mix_links_before(STEPS[-1].t + 1 if layer else GROUPS))
                else:
                    sp.wait_ge(piece_empty["v"], PIECE.emptied(("out", layer, c - 2, NB - 1), "v"))
                src = (x2d, x1_dram)[layer]
                if layer == 1:
                    sp.wait_ge(x1_out, 16 * OUT_JOBS)
                sp.dma_start(res[c % 2], src.rearrange("(n i) d -> i n d", n=NB)[:, :, c * OUT_COLS:(c + 1) * OUT_COLS]).then_inc(res_in[c % 2], 16)

            for n in range(NB):
                sp.dma_start(xr[:, n, :], x2d[n * P:(n + 1) * P, :]).then_inc(x_in[n], 16)
                if n == 3:
                    raw(JOBS[0])
            sp.dma_start(gain[:, :, :], gains).then_inc(small_in, 16)
            sp.dma_start(sink[:, :], sinks_0.rearrange("(o h) -> o h", o=1).broadcast_to([P, H])).then_inc(small_in, 16)
            sp.dma_start(pos_i[:, :, :], positions).then_inc(small_in, 16)
            for layer in (0, 1):
                steps = LAYER_STEPS[layer]
                if layer == 1:
                    raw(("qkv", steps[0].t))
                for s in steps:
                    before = None if s.first else STEPS[s.t - 1]
                    if s.first:
                        raw(JOBS[JOB[("qkv", s.t)] + 1])
                    for slot in range(UNITS):
                        if (s.t, slot) in SLOT_RAW:
                            following = JOB[SLOT_RAW[s.t, slot]] + 1
                            raw(JOBS[following])
                        if before is not None:
                            if slot == 1 and layer == 1:
                                stats_out(before)
                                if before.ends_group:
                                    stats_in(before)
                            if before.ends_group:
                                if slot == LATE_C:
                                    coef_store(before)
                                    for k in range(2):
                                        coef_load(before, k)
                                at = slot - MIX_AT[layer]
                                if 0 <= at and at + 2 < len(mix_items(before)):
                                    coef_load(before, at + 2)
                                if at == len(mix_items(before)):
                                    mix_store(before)
                last = steps[-1]
                for k in range(3):
                    mix_load(layer, k)
                if layer == 1:
                    stats_out(last)
                    stats_in(last)
                raw(("out", layer, 1))
                for k in range(3, MIX_LOADS):
                    mix_load(layer, k)
                coef_store(last)
                for k in range(len(mix_items(last))):
                    coef_load(last, k)
                res_load(layer, 0)
                res_load(layer, 1)
                if layer == 1:
                    sp.wait_ge(mix_lo, 2 * (MIX_LOADS + 2))
                    sp.wait_ge(mix_hi, 2 * (MIX_LOADS + 2))
                    sp.dma_start(gain_row, final_norm.rearrange("(o d) -> o d", o=1).broadcast_to([P, D])).then_inc(gain_in, 16)
                for c in range(OUT_JOBS):
                    if c >= 1 and c + 1 < OUT_JOBS:
                        raw(("out", layer, c + 1))
                    if layer == 0:
                        sp.wait_ge(piece_empty["v"], PIECE.emptied(("out", 0, c, NB - 1), "v"))
                        cols = slice(c * OUT_COLS, (c + 1) * OUT_COLS)
                        sp.dma_start(x1_dram.rearrange("(n i) d -> i n d", n=NB)[:, :, cols], xr[:, :, cols]).then_inc(x1_out, 16)
                    if c + 2 < OUT_JOBS:
                        res_load(layer, c + 2)
            for n in range(NB):
                sp.wait_ge(xn_done, 2 * NB + n + 1)
                sp.dma_start(out2d[n * P:(n + 1) * P, :], xr[:, n, :]).then_inc(final_out, 16)
            sp.wait_ge(final_out, 16 * NB)

        @block.gpsimd
        def _(pool):
            pool.memset(ident[:, :], 0.0).then_inc(const_link, 1)
            pool.memset(masks[:, :, :], 0.0).then_inc(const_link, 1)
            pool.memset(no_sink[:, :], BIG).then_inc(const_link, 1)
            pool.wait_ge(const_link, 2)
            pool.affine_select(out=ident[:, :], in_=ident[:, :], compare_op=ALU.not_equal, fill=1.0, base=0,
                               pattern=[[-1, P]], channel_multiplier=1).then_inc(const_link, 1)
            for m in (2, 3):
                own = masks[:, m, :]
                pool.affine_select(out=own, in_=own, compare_op=ALU.is_ge, fill=MASKED, base=0,
                                   pattern=[[-1, P]], channel_multiplier=1).then_inc(const_link, 1)
            for m in (0, 1):
                prev = masks[:, m, :]
                pool.affine_select(out=prev, in_=prev, compare_op=ALU.is_ge, fill=MASKED, base=-m,
                                   pattern=[[1, P]], channel_multiplier=-1).then_inc(const_link, 1)
            pool.iota(parity[:, :], pattern=[[1, P]], base=0, channel_multiplier=1).then_inc(const_link, 1)
            pool.wait_ge(const_link, 9)
            pool.sem_inc(consts, 1)

            def w_lo(job, q):
                pool.wait_ge(w_hi_done, 4 * JOB[job] + q + 1)
                hi = weights(job, 0)[:, 2 * q:2 * q + 2, :]
                lo = weights(job, 1)[:, 2 * q:2 * q + 2, :]
                cols = hi.shape[2]
                pool.tensor_tensor(lo, w_raw[:, 2 * q:2 * q + 2, 0:cols], hi.bitcast(F32), ALU.subtract).then_inc(w_lo_done["p"], 1)

            def rotate(t, half):
                p = STEPS[t].p
                for k in (4 * half + 2, 4 * half + 3):
                    wait_piece_emptied(pool, ("qkv", t, k))
                if t == 0 and half == 0:
                    pool.wait_ge(tables, 1)
                for i in range(2):
                    base = 4 * (4 * t + 2 * half + i)
                    if base > 0:
                        pool.wait_ge(rot_link, base)
                    rows = slice(4 * half + 2 * i, 4 * half + 2 * i + 2)
                    xs = qk[:, rows, :].rearrange("p n (h c) -> p n h c", c=HD)
                    cos = cosines[:, p, rows, :].rearrange("p n (o c) -> p n o c", o=1).broadcast_to([P, 2, 6, ROT])
                    sin = sines[:, p, rows, :].rearrange("p n (o c) -> p n o c", o=1).broadcast_to([P, 2, 6, ROT])
                    lower, upper = slice(0, HALF_ROT), slice(HALF_ROT, ROT)
                    pool.tensor_tensor(rot[:, :, :, lower], xs[:, :, :, upper], sin[:, :, :, lower], ALU.mult).then_inc(rot_link, 1)
                    pool.tensor_tensor(rot[:, :, :, upper], xs[:, :, :, lower], sin[:, :, :, upper], ALU.mult).then_inc(rot_link, 1)
                    pool.wait_ge(rot_link, base + 2)
                    pool.tensor_tensor(xs[:, :, :, 0:ROT], xs[:, :, :, 0:ROT], cos, ALU.mult).then_inc(rot_link, 1)
                    pool.wait_ge(rot_link, base + 3)
                    last = pool.tensor_tensor(xs[:, :, :, 0:ROT], xs[:, :, :, 0:ROT], rot[:, :, :, :], ALU.add).then_inc(rot_link, 1)
                pool.wait_ge(rot_link, base + 4)
                pool.sem_inc(rotated, 1)

            for layer in (0, 1):
                steps = LAYER_STEPS[layer]
                for q in (1, 3):
                    w_lo(("qkv", steps[0].t), q)
                for half in range(2):
                    rotate(steps[0].t, half)
                for s in steps:
                    pieces = [slot for slot in range(UNITS) for x_ in SLOT_PIECES.get((s.t, slot), []) if x_[0] == "qkv"]
                    for slot in range(UNITS):
                        if (s.t, slot) in SLOT_SPLIT:
                            job, q = SLOT_SPLIT[s.t, slot]
                            if q % 2 == 1:
                                w_lo(job, q)
                        if not s.last and slot == pieces[3] + 1:
                            rotate(s.t + 1, 0)
                        if not s.last and slot == min(pieces[7] + 1, UNITS - 1):
                            rotate(s.t + 1, 1)
                for c in range(OUT_JOBS):
                    for q in (1, 3):
                        w_lo(("out", layer, c), q)

        @block.tensor
        def _(pe):
            def free_bank(ring, empty, key):
                for e, count in ring.free(key):
                    pe.wait_ge(empty[e], count)

            def norm_piece(layer, kt, half):
                key = ("norm", layer, kt, half)
                free_bank(PIECE, piece_empty, key)
                pe.wait_ge(xn_done, layer * NB + 4 * half + 4)
                for i in range(4):
                    last = pe.transpose(j_bank[PIECE.bank(key)][:, i * P:(i + 1) * P],
                                        xr[:, 4 * half + i, kt * P:(kt + 1) * P], ident[:, :])
                last.then_inc(piece_full, 1)

            def wait_weights(job):
                for e in "vp":
                    pe.wait_ge(w_lo_done[e], 2 * (JOB[job] + 1))

            def piece(key):
                job, k = key[:-1], key[-1]
                free_bank(PIECE, piece_empty, key)
                if k == 0:
                    wait_weights(job)
                if job[0] == "qkv":
                    s = STEPS[job[1]]
                    if s.first:
                        wait_piece_emptied(pe, ("norm", s.layer, KT - 1, k // 4))
                    a = [[block_positions(ht[i][:, kt, :], s.p, k) for kt in range(KT)] for i in range(2)]
                    b = [[weights(job, i)[:, kt, :] for kt in range(KT)] for i in range(2)]
                    to = j_bank[PIECE.bank(key)][:, 0:QKV]
                elif job[0] == "gate":
                    r, half = k // 2, k % 2
                    a = [[weights(job, i)[:, kt, r * P:(r + 1) * P] for kt in range(KT)] for i in range(2)]
                    b = [[ht[i][:, kt, half * 512:(half + 1) * 512] for kt in range(KT)] for i in range(2)]
                    to = j_bank[PIECE.bank(key)][:, :]
                else:
                    if job[2] == 0 and k == 0:
                        pe.wait_ge(mix_lo, (job[1] + 1) * (MIX_LOADS + 2))
                        pe.wait_ge(mix_hi, (job[1] + 1) * (MIX_LOADS + 2))
                    a = [[ht[i][:, kt, k * P:(k + 1) * P] for kt in range(KT)] for i in range(2)]
                    b = [[weights(job, i)[:, kt, :] for kt in range(KT)] for i in range(2)]
                    to = j_bank[PIECE.bank(key)][:, 0:OUT_COLS]
                for kt in range(KT):
                    for x_, y_ in ((0, 0), (0, 1), (1, 0)):
                        last = pe.matmul(to, a[x_][kt], b[y_][kt], start=(kt == 0 and x_ == 0 and y_ == 0),
                                         stop=(kt == KT - 1 and x_ == 1))
                last.then_inc(piece_full, 1)
                pieces = 4 if job[0] == "gate" else NB
                if k == pieces - 1:
                    pe.wait_ge(piece_full, PIECE.filled(key))
                    pe.sem_inc(job_done, 1)

            def fill(t, what, half):
                key = (t, what, half)
                free_bank(TURN, turn_empty, key)
                pe.wait_ge(rotated, 2 * t + half + 1)
                c0 = R * HD if what == "K" else int(what[1]) * P
                for i in range(4):
                    last = pe.transpose(t_bank[TURN.bank(key)][:, i * P:(i + 1) * P],
                                        qk[:, 4 * half + i, c0:c0 + P], ident[:, :])
                last.then_inc(turned, 1)

            def score(s, u):
                r, n = u // NB, u % NB
                i = UNITS * s.t + u
                if i >= 2:
                    pe.wait_ge(biased, i - 1)
                if n % 4 == 0:
                    wait_turn_emptied(pe, (s.t, "K", n // 4))
                    wait_turn_emptied(pe, (s.t, f"Q{r}", n // 4))
                lo = 0 if s.has_prev(n) else P
                for j in range(2):
                    to = s_bank[i % 2][:, 2 * P * j + lo:2 * P * (j + 1)]
                    for part in range(2):
                        last = pe.matmul(to, qs[:, 2 * r + j, n * P:(n + 1) * P],
                                         ks[:, part, (n - 1) * P + lo:(n + 1) * P], start=(part == 0), stop=(part == 1))
                last.then_inc(scored, 1)

            def turn(s, u):
                r, n = u // NB, u % NB
                i = UNITS * s.t + u
                key = (s.t, u)
                free_bank(TURN, turn_empty, key)
                pe.wait_ge(exped, i + 1)
                for j in range(2):
                    for side in range(0 if s.has_prev(n) else 1, 2):
                        last = pe.transpose(t_bank[TURN.bank(key)][:, (2 * j + side) * P:(2 * j + side + 1) * P],
                                            probs[:, i % PROBS, j, side, :], ident[:, :])
                last.then_inc(turned, 1)

            def times_v(s, u):
                r, n = u // NB, u % NB
                i = UNITS * s.t + u
                group = 4 * s.t + 2 * r + n // 4
                wait_turn_emptied(pe, (s.t, u))
                if n % 4 == 0:
                    if group >= 2:
                        pe.wait_ge(ot_stored, group - 1)
                if u == 0 or u == 4:
                    for k in (4 * (u // 4) + 2, 4 * (u // 4) + 3):
                        wait_piece_emptied(pe, ("qkv", s.t, k))
                sides = [0, 1] if s.has_prev(n) else [1]
                for side in sides:
                    for j in range(2):
                        last = pe.matmul(o_bank[group % 2][64 * j:64 * j + 64, (n % 4) * P:(n % 4 + 1) * P],
                                         v[:, s.t % 2, n - 1 + side, :], probs_t[:, i % 2, 2 * j + side, :],
                                         start=(side == sides[0]), stop=(side == 1))
                last.then_inc(summed, 1)

            def coef_turn(s):
                key = ("C", s.t)
                rows = (1 if s.layer == 0 else 3) * NB * R
                free_bank(TURN, turn_empty, key)
                pe.wait_ge(den_v, links_before(s.t) + links_per_group(s.layer))
                src = comb[:, 1 - s.layer, :, :, :].rearrange("p a b c -> p (a b c)")[:, 0:rows]
                pe.transpose(t_bank[TURN.bank(key)][0:rows, 0:P], src, ident[:, :]).then_inc(turned, 1)

            pe.wait_ge(consts, 1)
            for layer in (0, 1):
                steps = LAYER_STEPS[layer]
                for kt in range(KT):
                    norm_piece(layer, kt, 0)
                for k in range(NB):
                    piece(("qkv", steps[0].t, k))
                    if k < 4:
                        for kt in (2 * k, 2 * k + 1):
                            norm_piece(layer, kt, 1)
                for what, half in FILLS_BEFORE.values():
                    fill(steps[0].t, what, half)
                for s in steps:
                    for slot in range(UNITS):
                        score(s, slot)
                        for key in SLOT_PIECES.get((s.t, slot), []):
                            piece(key)
                        b, u = unit_before(s, slot, 1)
                        if b:
                            turn(b, u)
                        if slot in FILLS_WITHIN:
                            fill(s.t, *FILLS_WITHIN[slot])
                        if slot in FILLS_BEFORE and not s.last:
                            fill(s.t + 1, *FILLS_BEFORE[slot])
                        if slot == LATE_C and not s.first and STEPS[s.t - 1].ends_group:
                            coef_turn(STEPS[s.t - 1])
                        b, u = unit_before(s, slot, 2)
                        if b:
                            times_v(b, u)
                last = steps[-1]
                turn(last, UNITS - 1)
                times_v(last, UNITS - 2)
                times_v(last, UNITS - 1)
                coef_turn(last)
                for c in range(OUT_JOBS):
                    for k in range(NB):
                        piece(("out", layer, c, k))

        @block.scalar
        def _(act):
            def w_hi(job, q):
                n = JOB[job]
                act.wait_ge(raw_in, 16 * (n + 1))
                before = previous_in_buffer(job)
                if q == 0 and before >= 0:
                    act.wait_ge(job_done, before + 1)
                if q == 0 and second_buffer(job):
                    act.wait_ge(scored, UNITS * (LAYER_STEPS[job[1]][-1].t + 1))
                to = weights(job, 0)[:, 2 * q:2 * q + 2, :]
                act.activation(to, w_raw[:, 2 * q:2 * q + 2, 0:to.shape[2]], ACT.Copy).then_inc(w_hi_done, 1)

            def exps(s, u):
                r, n = u // NB, u % NB
                i = UNITS * s.t + u
                lo = 0 if s.has_prev(n) else P
                act.wait_ge(biased, i + 1)
                for j in range(2):
                    h = 2 * r + j
                    row = probs[:, i % PROBS, j, lo // P:2, :]
                    last = act.activation(row, row, ACT.Exp, bias=stat[:, s.t % 2, n, h:h + 1], scale=SCALE,
                                          accum_out=stat[:, s.t % 2, n, R + h:R + h + 1])
                last.then_inc(exped, 1)

            def empty_piece(key):
                if "a" not in PIECE.uses[PIECE.at[key]]:
                    return
                act.wait_ge(piece_full, PIECE.filled(key))
                src = j_bank[PIECE.bank(key)]
                if key[0] == "qkv":
                    k = key[2]
                    guard_qkv(act, key)
                    act.activation(qk[:, k, 0:R * HD + HD], src[:, 0:R * HD + HD], ACT.Copy)
                    act.activation(qk[:, k, R * HD + HD:], src[:, R * HD:R * HD + HD], ACT.Copy)
                    last = act.activation(v[:, key[1] % 2, k, :], src[:, R * HD + HD:QKV], ACT.Copy)
                elif key[0] == "gate":
                    r, half = key[3] // 2, key[3] % 2
                    guard_gate(act, key)
                    last = act.activation(gate[:, r, half * 512:(half + 1) * 512], src[:, :], ACT.Copy)
                last.then_inc(piece_empty["a"], 1)

            def empty_norm(layer, kt, half):
                key = ("norm", layer, kt, half)
                act.wait_ge(piece_full, PIECE.filled(key))
                act.activation(ht[0][:, kt, half * 512:(half + 1) * 512], j_bank[PIECE.bank(key)][:, :], ACT.Copy,
                               scale=gain[:, layer, kt:kt + 1]).then_inc(piece_empty["a"], 1)

            def empty_turn(s, u):
                if u % 2 == 0:
                    store_turn(act, act.copy, s, u).then_inc(turn_empty["a"], 1)

            def fill_hi(t, what, half):
                key = (t, what, half)
                act.wait_ge(turned, TURN.filled(key))
                guard_fill(act, t, what, half)
                src = t_bank[TURN.bank(key)]
                cols = slice(half * 512, (half + 1) * 512)
                if what == "K":
                    last = act.activation(ks[:, 0, cols], src[:, :], ACT.Copy)
                else:
                    h = 2 * int(what[1])
                    act.activation(qs[0:64, h, cols], src[0:64, :], ACT.Copy)
                    last = act.activation(qs[64:P, h + 1, cols], src[64:P, :], ACT.Copy)
                last.then_inc(turn_empty["a"], 1)

            def silu(s):
                for k in range(4):
                    wait_piece_emptied(act, ("gate", s.layer, s.g, k))
                act.activation(gate[:, :, :], gate[:, :, :], ACT.Silu).then_inc(silued, 1)

            def den_exp(s):
                n = links_before(s.t)
                if s.layer == 0:
                    act.wait_ge(den_v, n + 1)
                    e = comb[:, 0, 0, :, :]
                else:
                    act.wait_ge(den_v, n + 3)
                    e = comb[:, 0, :, :, :]
                act.activation(e, e, ACT.Exp).then_inc(den_a, 1)

            def mix_split(layer, k, src):
                act.activation(ht[0][:, k, :], src, ACT.Copy).then_inc(mix_hi, 1)

            def squares(base, wait):
                for n in range(0, NB, 2):
                    wait(act, n)
                    if base + n // 2 > 0:
                        act.wait_ge(squared["a"], base + n // 2)
                    act.activation(square_a, xr[:, n, :], ACT.Square, accum_out=sums[:, n:n + 1]).then_inc(squared["a"], 1)

            def root(k):
                act.wait_ge(norm_v, NORM_LINKS * k + 1)
                act.activation(ssq[:, 1, :], ssq[:, 0, :], ACT.Sqrt).then_inc(norm_a, 1)

            act.wait_ge(rope_v, ROPE_LINKS)
            act.activation(rope_w[:, 1, :], rope_w[:, 0, :], ACT.Sin).then_inc(rope_a, 1)
            act.activation(rope_w[:, 2, :], rope_w[:, 0, :], ACT.Sin, scale=0.5).then_inc(rope_a, 1)
            for layer in (0, 1):
                steps = LAYER_STEPS[layer]
                for q in range(4):
                    if layer == 0:
                        w_hi(("qkv", steps[0].t), q)
                squares(layer * 4, row_ready(layer))
                root(layer)
                if layer == 1:
                    for q in range(4):
                        w_hi(("qkv", steps[0].t), q)
                for kt in range(KT):
                    empty_norm(layer, kt, 0)
                for k in range(NB):
                    empty_piece(("qkv", steps[0].t, k))
                    if k < 4:
                        for kt in (2 * k, 2 * k + 1):
                            empty_norm(layer, kt, 1)
                for what, half in FILLS_BEFORE.values():
                    fill_hi(steps[0].t, what, half)
                for s in steps:
                    before = None if s.first else STEPS[s.t - 1]
                    for slot in range(UNITS):
                        if (s.t, slot) in SLOT_SPLIT:
                            w_hi(*SLOT_SPLIT[s.t, slot])
                        if slot == 2 and before is not None and before.ends_group:
                            silu(before)
                        exps(s, slot)
                        for key in SLOT_PIECES.get((s.t, slot), []):
                            empty_piece(key)
                        b, u = unit_before(s, slot, 1)
                        if b:
                            empty_turn(b, u)
                        if slot in FILLS_WITHIN:
                            fill_hi(s.t, *FILLS_WITHIN[slot])
                        if slot in FILLS_BEFORE and not s.last:
                            fill_hi(s.t + 1, *FILLS_BEFORE[slot])
                        if slot == (1 if layer == 0 else 3) and before is not None and before.ends_group:
                            den_exp(before)
                last = steps[-1]
                empty_turn(last, UNITS - 1)
                if layer == 0:
                    den_exp(last)
                for q in range(4):
                    w_hi(("out", layer, 0), q)
                act.wait_ge(job_done, JOB[("gate", layer, GROUPS - 1)] + 1)
                for k in range(MIX_LOADS):
                    if layer == 1 and k == 1:
                        den_exp(last)
                    act.wait_ge(mix_back[k % 3], 16 * (layer * 2 + k // 3 + 1))
                    mix_split(layer, k, mix_in[k % 3])
                silu(last)
                for q in range(4):
                    w_hi(("out", layer, 1), q)
                act.wait_ge(mixed, mix_links_before(last.t) + mix_links(last))
                for r in range(2):
                    mix_split(layer, MIX_LOADS + r, ot[out_region(last)][:, r, :])
                for c in range(2, OUT_JOBS):
                    for q in range(4):
                        w_hi(("out", layer, c), q)
            squares(8, row_ready(2))
            root(2)

        @block.vector
        def _(dve):
            def w_lo(job, q):
                dve.wait_ge(w_hi_done, 4 * JOB[job] + q + 1)
                hi = weights(job, 0)[:, 2 * q:2 * q + 2, :]
                lo = weights(job, 1)[:, 2 * q:2 * q + 2, :]
                dve.tensor_tensor(lo, w_raw[:, 2 * q:2 * q + 2, 0:hi.shape[2]], hi.bitcast(F32), ALU.subtract).then_inc(w_lo_done["v"], 1)

            def mask_of(s, n):
                if s.layer == 1 and s.p == 2:
                    return masks[:, 3:4, :]
                if not s.has_prev(n):
                    return masks[:, 2:3, :]
                return masks[:, 1:3, :] if s.layer == 0 else masks[:, 0:3:2, :]

            def mask_max(s, u):
                r, n = u // NB, u % NB
                i = UNITS * s.t + u
                lo = 0 if s.has_prev(n) else P
                dve.wait_ge(scored, i + 1)
                if i >= PROBS:
                    b = i - PROBS
                    dve.wait_ge(turned, TURN.filled((b // UNITS, b % UNITS)))
                if u == 0 and s.layer == 1 and s.t >= GROUPS + 2:
                    dve.wait_ge(stat_out[s.t % 2], stat_stored(s.t - 2))
                for j in range(2):
                    src = s_bank[i % 2][:, 2 * P * j:2 * P * (j + 1)].rearrange("p (e k) -> p e k", e=2)
                    last = dve.tensor_tensor_reduce(probs[:, i % PROBS, j, lo // P:2, :], src[:, lo // P:2, :], mask_of(s, n),
                                                    1.0, -BIG, ALU.add, ALU.max, mx[:, i % 2, j:j + 1])
                last.then_inc(masked, 1)
                dve.wait_ge(masked, i + 1)
                least = neg_sink[:, R * s.g + 2 * r:R * s.g + 2 * r + 2] if s.layer == 0 else no_sink[:, :]
                dve.scalar_tensor_tensor(out=stat[:, s.t % 2, n, 2 * r:2 * r + 2], in0=mx[:, i % 2, :], scalar=-SCALE,
                                         in1=least, op0=ALU.mult, op1=ALU.min).then_inc(biased, 1)

            def empty_piece(key):
                if "v" not in PIECE.uses[PIECE.at[key]]:
                    return
                dve.wait_ge(piece_full, PIECE.filled(key))
                src = j_bank[PIECE.bank(key)]
                if key[0] == "qkv":
                    k = key[2]
                    guard_qkv(dve, key)
                    dve.tensor_copy(qk[:, k, 0:R * HD + HD], src[:, 0:R * HD + HD])
                    dve.tensor_copy(qk[:, k, R * HD + HD:], src[:, R * HD:R * HD + HD])
                    last = dve.tensor_copy(v[:, key[1] % 2, k, :], src[:, R * HD + HD:QKV])
                elif key[0] == "gate":
                    r, half = key[3] // 2, key[3] % 2
                    guard_gate(dve, key)
                    last = dve.tensor_copy(gate[:, r, half * 512:(half + 1) * 512], src[:, :])
                else:
                    _, layer, c, k = key
                    if k == 0:
                        dve.wait_ge(res_in[c % 2], 16 * (2 * layer + c // 2 + 1))
                    last = dve.tensor_tensor(xr[:, k, c * OUT_COLS:(c + 1) * OUT_COLS], src[:, 0:OUT_COLS],
                                             res[c % 2][:, k, :], ALU.add)
                last.then_inc(piece_empty["v"], 1)

            def empty_norm(layer, kt, half):
                key = ("norm", layer, kt, half)
                cols = slice(half * 512, (half + 1) * 512)
                dve.wait_ge(piece_full, PIECE.filled(key))
                dve.wait_ge(piece_empty["a"], PIECE.emptied(key, "a"))
                dve.scalar_tensor_tensor(out=ht[1][:, kt, cols], in0=j_bank[PIECE.bank(key)][:, :],
                                         scalar=gain[:, layer, kt:kt + 1], in1=ht[0][:, kt, cols].bitcast(F32),
                                         op0=ALU.mult, op1=ALU.subtract).then_inc(piece_empty["v"], 1)

            def empty_turn(s, u):
                if u % 2 == 1:
                    store_turn(dve, dve.tensor_copy, s, u).then_inc(turn_empty["v"], 1)

            def fill_lo(t, what, half):
                key = (t, what, half)
                dve.wait_ge(turn_empty["a"], TURN.emptied(key, "a"))
                guard_fill(dve, t, what, half)
                src = t_bank[TURN.bank(key)]
                cols = slice(half * 512, (half + 1) * 512)
                if what == "K":
                    last = dve.tensor_tensor(ks[:, 1, cols], src[:, :], ks[:, 0, cols].bitcast(F32), ALU.subtract)
                else:
                    h = 2 * int(what[1])
                    dve.tensor_tensor(qs[64:P, h, cols], src[0:64, :], qs[0:64, h, cols].bitcast(F32), ALU.subtract)
                    last = dve.tensor_tensor(qs[0:64, h + 1, cols], src[64:P, :], qs[64:P, h + 1, cols].bitcast(F32), ALU.subtract)
                last.then_inc(turn_empty["v"], 1)

            def store_ot(s, r, half):
                group = 4 * s.t + 2 * r + half
                dve.wait_ge(summed, UNITS * s.t + NB * r + 4 * half + 4)
                if s.layer == 1 and r == 0 and half == 0:
                    done = GROUPS - 1 + sum(q.ends_group for q in STEPS[GROUPS:s.t - s.p]) - (s.p == 0 and s.g > 0)
                    dve.wait_ge(mix_out, 32 * done)
                to = patterned(ot[s.t % 4][:, r, :], s.p, half)
                src = o_bank[group % 2][:, :].rearrange("a (b c) -> a b c", b=to.shape[1])
                dve.tensor_copy(to, src).then_inc(ot_stored, 1)

            def link(ins, sem_, value):
                ins.then_inc(sem_, 1)
                dve.wait_ge(sem_, value)

            def coefs_first(s):
                n = links_before(s.t)
                dve.wait_ge(exped, UNITS * (s.t + 1))
                if groups_before(s.t) > 0:
                    before = [q.t for q in STEPS[:s.t] if q.ends_group][-1]
                    dve.wait_ge(turned, TURN.filled(("C", before)))
                if s.layer == 0:
                    sinks = sink[:, R * s.g:R * (s.g + 1)].rearrange("p (o h) -> p o h", o=1).broadcast_to([P, NB, R])
                    link(dve.tensor_tensor(comb[:, 0, 0, :, :], stat[:, s.t % 2, :, 0:R], sinks, ALU.add), den_v, n + 1)
                    return
                dve.wait_ge(nat_in, 48 * (s.g + 1))
                least = comb_small[:, 0, :, :]
                link(dve.tensor_tensor(least, nat[:, 0, :, 0:R], nat[:, 1, :, 0:R], ALU.min), den_v, n + 1)
                link(dve.tensor_tensor(least, least, nat[:, 2, :, 0:R], ALU.min), den_v, n + 2)
                for p in range(3):
                    last = dve.tensor_tensor(comb[:, 0, p, :, :], least, nat[:, p, :, 0:R], ALU.subtract)
                link(last, den_v, n + 3)

            def coefs_last(s):
                n = links_before(s.t)
                dve.wait_ge(den_a, groups_before(s.t) + 1)
                if s.layer == 0:
                    link(dve.tensor_tensor(comb_small[:, 0, :, :], comb[:, 0, 0, :, :], stat[:, s.t % 2, :, R:2 * R], ALU.add), den_v, n + 2)
                    link(dve.reciprocal(comb[:, 1, 0, :, :], comb_small[:, 0, :, :]), den_v, n + 3)
                    dve.sem_inc(den_v, 1)
                    return
                for p in range(3):
                    last = dve.tensor_tensor(comb[:, 1, p, :, :], comb[:, 0, p, :, :], nat[:, p, :, R:2 * R], ALU.mult)
                link(last, den_v, n + 4)
                link(dve.tensor_tensor(comb[:, 1, 0, :, :], comb[:, 1, 0, :, :], comb[:, 1, 1, :, :], ALU.add), den_v, n + 5)
                link(dve.tensor_tensor(comb[:, 1, 0, :, :], comb[:, 1, 0, :, :], comb[:, 1, 2, :, :], ALU.add), den_v, n + 6)
                dve.reciprocal(comb_small[:, 1, :, :], comb[:, 1, 0, :, :]).then_inc(norm_r, 1)
                dve.wait_ge(norm_r, s.g + 1)
                for p in range(3):
                    last = dve.tensor_tensor(comb[:, 0, p, :, :], comb[:, 0, p, :, :], comb_small[:, 1, :, :], ALU.mult)
                link(last, den_v, n + 7)

            def coef_store(s):
                key = ("C", s.t)
                rows = (1 if s.layer == 0 else 3) * NB * R
                dve.wait_ge(turned, TURN.filled(key))
                if groups_before(s.t) > 0:
                    dve.wait_ge(coef_out, 16 * groups_before(s.t))
                dve.tensor_copy(coef_rows[0:rows, :], t_bank[TURN.bank(key)][0:rows, 0:P]).then_inc(turn_empty["v"], 1)

            def mix(s, k):
                items = mix_items(s)
                r, p = items[k]
                index = coef_loads_before(s.t) + k
                done = product_link(index)
                region = out_region(s)
                tile = ot[(region + p) % 4][:, r, :]
                into = ot[region][:, r, :]
                dve.wait_ge(coef_in[index % 2], 32 * (index // 2 + 1))
                dve.wait_ge(ot_stored, 4 * (s.t + 1))
                link(dve.tensor_tensor(tile, tile, coef[:, index % 2, :], ALU.mult), mixed, done)
                if p > 0:
                    done += 1
                    link(dve.tensor_tensor(into, into, tile, ALU.add), mixed, done)
                if k + 1 == len(items) or items[k + 1][0] != r:
                    dve.wait_ge(silued, groups_before(s.t) + 1)
                    link(dve.tensor_tensor(into, into, gate[:, r, :], ALU.mult), mixed, done + 1)

            def mix_split(layer, k, src):
                dve.wait_ge(mix_hi, layer * (MIX_LOADS + 2) + k + 1)
                dve.tensor_tensor(ht[1][:, k, :], src, ht[0][:, k, :].bitcast(F32), ALU.subtract).then_inc(mix_lo, 1)

            def squares(base, wait):
                for n in range(1, NB, 2):
                    wait(dve, n)
                    if base + n // 2 > 0:
                        dve.wait_ge(squared["v"], base + n // 2)
                    dve.tensor_tensor_reduce(square_v, xr[:, n, :], xr[:, n, :], 1.0, 0.0, ALU.mult, ALU.add,
                                             sums[:, n:n + 1]).then_inc(squared["v"], 1)

            def inverse_rms(k):
                base = NORM_LINKS * k
                var, y, z = ssq[:, 0, :], ssq[:, 2, :], ssq[:, 3, :]
                dve.wait_ge(squared["a"], 4 * (k + 1))
                dve.wait_ge(squared["v"], 4 * (k + 1))
                link(dve.tensor_scalar(var, sums[:, :], 1.0 / D, EPS, ALU.mult, ALU.add), norm_v, base + 1)
                dve.wait_ge(norm_a, k + 1)
                link(dve.reciprocal(y, ssq[:, 1, :]), norm_v, base + 2)
                link(dve.tensor_tensor(z, y, y, ALU.mult), norm_v, base + 3)
                link(dve.tensor_tensor(z, z, var, ALU.mult), norm_v, base + 4)
                link(dve.tensor_scalar(z, z, -0.5, 1.5, ALU.mult, ALU.add), norm_v, base + 5)
                link(dve.tensor_tensor(y, y, z, ALU.mult), norm_v, base + 6)

            def rope_tables():
                n = [0]

                def chain(ins):
                    n[0] += 1
                    link(ins, rope_v, n[0])

                ang = rope_w[:, 0, :].rearrange("p (t j) -> p t j", j=HALF_ROT)
                turns = rope_w[:, 1, :]
                part = rope_w[:, 2, :]
                chain(dve.tensor_copy(pos_f[:, :, :], pos_i[:, :, :]))
                flat = pos_f[:, :, :].rearrange("p a b -> p (a b)")
                for j in range(HALF_ROT):
                    freq = float(np.float32(THETA ** (-j / HALF_ROT)))
                    last = dve.tensor_scalar(ang[:, :, j], flat, freq, None, ALU.mult)
                chain(last)
                magic = 1.5 * 2.0 ** 23
                for period in (2 * np.pi * 256, 2 * np.pi):
                    rest, parts = period, []
                    for bits in (9, 9):
                        unit = 2.0 ** (np.floor(np.log2(rest)) - bits + 1)
                        parts.append(np.floor(rest / unit) * unit)
                        rest -= parts[-1]
                    parts.append(rest)
                    chain(dve.tensor_scalar(turns, rope_w[:, 0, :], float(1.0 / period), magic, ALU.mult, ALU.add))
                    chain(dve.tensor_scalar(turns, turns, -magic, None, ALU.add))
                    for c in parts:
                        chain(dve.tensor_scalar(part, turns, float(c), None, ALU.mult))
                        chain(dve.tensor_tensor(rope_w[:, 0, :], rope_w[:, 0, :], part, ALU.subtract))
                for _ in range(ROPE_LINKS - 2 - 16 - 1):
                    dve.sem_inc(rope_v, 1)
                    n[0] += 1
                pi = float(np.nextafter(np.float32(np.pi), np.float32(0)))
                chain(dve.tensor_scalar(rope_w[:, 0, :], rope_w[:, 0, :], pi, -pi, ALU.min, ALU.max))
                dve.wait_ge(rope_a, 2)
                sin = rope_w[:, 1, :].rearrange("p (t j) -> p t j", j=HALF_ROT)
                half = rope_w[:, 2, :]
                cos_to = cosines[:, :, :, :].rearrange("p a b c -> p (a b) c")
                sin_to = sines[:, :, :, :].rearrange("p a b c -> p (a b) c")
                dve.tensor_copy(sin_to[:, :, HALF_ROT:ROT], sin)
                dve.tensor_scalar(sin_to[:, :, 0:HALF_ROT], sin, -1.0, None, ALU.mult)
                chain(dve.tensor_tensor(half, half, half, ALU.mult))
                halves = half.rearrange("p (t j) -> p t j", j=HALF_ROT)
                dve.tensor_scalar(cos_to[:, :, 0:HALF_ROT], halves, -2.0, 1.0, ALU.mult, ALU.add)
                chain(dve.tensor_scalar(cos_to[:, :, HALF_ROT:ROT], halves, -2.0, 1.0, ALU.mult, ALU.add))
                dve.sem_inc(tables, 1)

            dve.wait_ge(small_in, 16 * 3)
            rope_tables()
            dve.tensor_scalar(neg_sink[:, :], sink[:, :], -1.0, None, ALU.mult).then_inc(sink_neg, 1)
            dve.wait_ge(sink_neg, 1)
            dve.wait_ge(consts, 1)
            odd = gate[:, 1, P:2 * P]
            link(dve.tensor_scalar(parity[:, :], parity[:, :], 1, None, ALU.bitwise_and), mask_v, 1)
            link(dve.tensor_scalar(odd, parity[:, :], MASKED, None, ALU.mult), mask_v, 2)
            link(dve.tensor_tensor(masks[:, 3, :], masks[:, 3, :], odd, ALU.add), mask_v, 3)
            for layer in (0, 1):
                steps = LAYER_STEPS[layer]
                if layer == 0:
                    for q in (0, 2):
                        w_lo(("qkv", steps[0].t), q)
                squares(4 * layer, row_ready(layer))
                inverse_rms(layer)
                if layer == 1:
                    dve.wait_ge(x1_out, 16 * OUT_JOBS)
                for n in range(NB):
                    dve.tensor_scalar(xr[:, n, :], xr[:, n, :], ssq[:, 2, n:n + 1], None, ALU.mult).then_inc(xn_done, 1)
                if layer == 1:
                    for q in (0, 2):
                        w_lo(("qkv", steps[0].t), q)
                for kt in range(KT):
                    empty_norm(layer, kt, 0)
                for k in range(NB):
                    empty_piece(("qkv", steps[0].t, k))
                    if k < 4:
                        for kt in (2 * k, 2 * k + 1):
                            empty_norm(layer, kt, 1)
                for what, half in FILLS_BEFORE.values():
                    fill_lo(steps[0].t, what, half)
                for s in steps:
                    before = None if s.first else STEPS[s.t - 1]
                    for slot in range(UNITS):
                        mask_max(s, slot)
                        if (s.t, slot) in SLOT_SPLIT and SLOT_SPLIT[s.t, slot][1] % 2 == 0:
                            w_lo(*SLOT_SPLIT[s.t, slot])
                        for key in SLOT_PIECES.get((s.t, slot), []):
                            empty_piece(key)
                        b, u = unit_before(s, slot, 1)
                        if b:
                            empty_turn(b, u)
                        if slot in FILLS_WITHIN:
                            fill_lo(s.t, *FILLS_WITHIN[slot])
                        if slot in FILLS_BEFORE and not s.last:
                            fill_lo(s.t + 1, *FILLS_BEFORE[slot])
                        if before is not None and before.ends_group:
                            if slot == (1 if layer == 0 else 3):
                                coefs_first(before)
                            if slot == (2 if layer == 0 else 4):
                                coefs_last(before)
                            if slot == LATE_C:
                                coef_store(before)
                            at = slot - MIX_AT[layer]
                            if 0 <= at < len(mix_items(before)):
                                mix(before, at)
                        b, u = unit_before(s, slot, 2)
                        if b and u % 4 == 3:
                            store_ot(b, u // NB, (u % NB) // 4)
                last = steps[-1]
                empty_turn(last, UNITS - 1)
                store_ot(last, 1, 1)
                if layer == 0:
                    coefs_first(last)
                    coefs_last(last)
                    coef_store(last)
                for q in (0, 2):
                    w_lo(("out", layer, 0), q)
                for k in range(MIX_LOADS):
                    if layer == 1 and k == 1:
                        coefs_first(last)
                        coefs_last(last)
                        coef_store(last)
                    mix_split(layer, k, mix_in[k % 3])
                for q in (0, 2):
                    w_lo(("out", layer, 1), q)
                for k in range(len(mix_items(last))):
                    mix(last, k)
                for r in range(2):
                    mix_split(layer, MIX_LOADS + r, ot[out_region(last)][:, r, :])
                for c in range(OUT_JOBS):
                    if c >= 2:
                        for q in (0, 2):
                            w_lo(("out", layer, c), q)
                    for k in range(NB):
                        empty_piece(("out", layer, c, k))
            squares(8, row_ready(2))
            inverse_rms(2)
            dve.wait_ge(gain_in, 16)
            for n in range(NB):
                dve.scalar_tensor_tensor(out=xr[:, n, :], in0=xr[:, n, :], scalar=ssq[:, 2, n:n + 1], in1=gain_row,
                                         op0=ALU.mult, op1=ALU.mult).then_inc(xn_done, 1)


def by_block(a, p):
    if p == 0:
        return a.reshape(NB, P).T
    if p == 1:
        return a.reshape(2, P, 4).transpose(1, 2, 0).reshape(P, NB)
    return a.reshape(P, NB)


def by_partition(w):
    return w.reshape(KT, P, w.shape[1]).transpose(1, 0, 2).reshape(P, -1)


def kernel(**inputs):
    import concourse.bacc as bacc
    from concourse.bass_utils import run_bass_kernel_spmd

    a = {name: np.asarray(value) for name, value in inputs.items()}
    w_in = [a["w_in_0"], a["w_in_1"]]
    qkv = []
    for s in STEPS:
        base, w = s.p * PER, w_in[s.layer]
        q0, k0, v0 = base + s.g * R * HD, base + D + s.g * HD, base + D + KV + s.g * HD
        qkv.append(by_partition(np.concatenate([w[:, q0:q0 + R * HD], w[:, k0:k0 + HD], w[:, v0:v0 + HD]], axis=1)))
    gates = [w_in[layer][:, base + g * R * HD:base + (g + 1) * R * HD]
             for layer, base in ((0, PER), (1, 3 * PER)) for g in range(GROUPS)]
    outs = [a[name][:, c * OUT_COLS:(c + 1) * OUT_COLS] for name in ("w_out_0", "w_out_1") for c in range(OUT_JOBS)]
    arrays = {
        "x": a["x"],
        "positions": np.stack([by_block(a["positions"][0], p) for p in range(3)], axis=1),
        "gains": np.stack([a[name].reshape(KT, P).T for name in ("norm_0", "norm_1")], axis=1),
        "sinks_0": a["sinks_0"],
        "final_norm": a["final_norm"],
        "w_qkv": np.stack(qkv),
        "w_gate": np.stack([by_partition(w) for w in gates]),
        "w_out": np.stack([by_partition(w) for w in outs]),
    }
    arrays = {f"in_{name}": np.ascontiguousarray(value) for name, value in arrays.items()}
    nc = bacc.Bacc("TRN2", target_bir_lowering=False, num_devices=1)
    args = [nc.dram_tensor(name, value.shape, mybir.dt.from_np(value.dtype), kind="ExternalInput").ap()
            for name, value in arrays.items()]
    args.append(nc.dram_tensor("out_0", (1, S, D), F32, kind="ExternalOutput").ap())
    trunk(nc, *args)
    got = run_bass_kernel_spmd(nc, [arrays], core_ids=[0])
    return got.results[0]["out_0"]
```

```python
from contextlib import ExitStack

import numpy as np
import concourse.bass as bass
from concourse import mybir

F32 = mybir.dt.float32
F32R = mybir.dt.float32r
I32 = mybir.dt.int32
ALU = mybir.AluOpType
ACT = mybir.ActivationFunctionType

P = 128
S = 1024
D = 1024
KT = D // P
NB = S // P
HD = 64
HALF_ROT = 8
ROT = 2 * HALF_ROT
H = 16
GROUPS = 4
R = H // GROUPS
SCALE = HD ** -0.5
EPS = 1e-6
THETA = 500000.0
MASKED = -1e30
QKV = R * HD + 2 * HD
KV = GROUPS * HD
PER = D + 2 * KV
OUT_COLS = 256
OUT_JOBS = D // OUT_COLS
UNITS = 2 * NB
BIG = 3.0e38
PROBS = 2



class Step:
    def __init__(self, t, layer, g, p):
        self.t, self.layer, self.g, self.p = t, layer, g, p
        self.last = (g == GROUPS - 1) and (layer == 0 or p == 2)
        self.first = g == 0 and p == 0
        self.ends_group = layer == 0 or p == 2

    def has_prev(self, n):
        return (n > 0) if self.p == 0 else (n % 2 == 1) if self.p == 1 else False


STEPS = [Step(g, 0, g, 0) for g in range(GROUPS)]
STEPS += [Step(GROUPS + 3 * g + p, 1, g, p) for g in range(GROUPS) for p in range(3)]
LAYER_STEPS = [[s for s in STEPS if s.layer == layer] for layer in (0, 1)]

JOBS = []
SLOT_SPLIT = {}
SLOT_PIECES = {}
def JOB_OF(job):
    return JOBS.index(job)


for _layer in (0, 1):
    _steps = LAYER_STEPS[_layer]
    JOBS.append(("qkv", _steps[0].t))
    for _s in _steps:
        _t = _s.t
        _slots = []
        if not _s.last:
            JOBS.append(("qkv", _t + 1))
            _slots.append((JOBS[-1], [1, 2, 3, 4, 6, 7, 8, 9] if _s.ends_group else [1, 3, 5, 7, 9, 11, 13, 14]))
        if _s.ends_group:
            JOBS.append(("gate", _layer, _s.g))
            _slots.append((JOBS[-1], [1, 3, 4, 6] if _s.last else [11, 12, 14, 15]))
        for _job, _pieces in _slots:
            for _k, _slot in enumerate(_pieces):
                SLOT_PIECES.setdefault((_t, _slot), []).append(_job + (_k,))
        _now = [JOB_OF(_job) for _job, _ in _slots]
        _at = [(0, _now[0], (2, 3))]
        if len(_now) == 2:
            _at += [(4, _now[1], (0,)), (5, _now[1], (1,)), (10, _now[1], (2, 3))]
            _at += [(12, _now[1] + 1, (0,)), (13, _now[1] + 1, (1,))]
        elif _s.last:
            _at += [(4, _now[0] + 1, (0,)), (5, _now[0] + 1, (1,)), (8, _now[0] + 1, (2, 3))]
        else:
            _at += [(5, _now[0] + 1, (0,)), (8, _now[0] + 1, (1,))]
        for _slot, _n, _qs in _at:
            SLOT_SPLIT[_t, _slot] = [(_n, _q) for _q in _qs]
    for _c in range(OUT_JOBS):
        JOBS.append(("out", _layer, _c))
JOB = {job: n for n, job in enumerate(JOBS)}


def columns(job):
    return {"qkv": QKV, "gate": R * HD, "out": OUT_COLS}[job[0]]


def packed_index(job):
    return job[1] if job[0] == "qkv" else 4 * job[1] + job[2]


def half_slot(n, half):
    return (2 * n + half) % 3


FILLS_BEFORE = {13: ("K", 0), 14: ("Q0", 0), 15: ("Q1", 0)}
FILLS_WITHIN = {1: ("K", 1), 2: ("Q0", 1), 3: ("Q1", 1)}
LATE_C = 5
SPLIT_MIX = [8, 9, 10, 11, 14, 15]
EARLY = 6
SPARE = [2, 3, 4, 5]


def mix_items(s):
    return [(r, half, p) for r in range(2) for half in range(2) for p in range(1 if s.layer == 0 else 3)]


def mix_slot(s, k):
    return 7 + k if s.layer == 0 else 8 + k // 2


class Ring:

    def __init__(self):
        self.uses, self.at = [], {}

    def add(self, key, by):
        self.at[key] = len(self.uses)
        self.uses.append(by)

    def bank(self, key):
        return self.at[key] % 2

    def filled(self, key):
        return self.at[key] + 1

    def emptied(self, key, engine):
        return sum(engine in by for by in self.uses[: self.at[key] + 1])

    def free(self, key):
        k = self.at[key] - 2
        if k < 0:
            return []
        return [(e, sum(e in by for by in self.uses[: k + 1])) for e in "av" if any(e in by for by in self.uses[: k + 1])]


def unit_before(s, u, back):
    u -= back
    if u >= 0:
        return s, u
    return (None, None) if s.first else (STEPS[s.t - 1], u + UNITS)


PIECE = Ring()
TURN = Ring()
for _layer in (0, 1):
    _first = LAYER_STEPS[_layer][0]
    for _k in range(NB):
        PIECE.add(("qkv", _first.t, _k), "av"[_k % 2])
    for _what, _half in FILLS_BEFORE.values():
        TURN.add((_first.t, _what, _half), "av")
    for _s in LAYER_STEPS[_layer]:
        for _slot in range(UNITS):
            for _n, _piece in enumerate(SLOT_PIECES.get((_s.t, _slot), [])):
                PIECE.add(_piece, "av"[_piece[-1] % 2])
            _b, _u = unit_before(_s, _slot, 1)
            if _b:
                TURN.add((_b.t, _u), "av"[_u % 2])
            if _slot in FILLS_WITHIN:
                TURN.add((_s.t,) + FILLS_WITHIN[_slot], "av")
            if _slot in FILLS_BEFORE and not _s.last:
                TURN.add((_s.t + 1,) + FILLS_BEFORE[_slot], "av")
            if _slot == LATE_C and not _s.first and STEPS[_s.t - 1].ends_group:
                TURN.add(("C", _s.t - 1), "v")
    TURN.add((_s.t, UNITS - 1), "av"[(UNITS - 1) % 2])
    TURN.add(("C", _s.t), "v")
    for _c in range(OUT_JOBS):
        for _k in range(NB):
            if _c > 0 or _k not in SPARE:
                PIECE.add(("out", _layer, _c, _k), "v")


def patterned(view, p, half):
    if p == 0:
        return view[:, half * 512:(half + 1) * 512].rearrange("a (b c) -> a b c", b=1)
    f = 4 if p == 1 else 8
    return view.rearrange("a (i f) -> a f i", f=f)[:, half * (f // 2):(half + 1) * (f // 2), :]


def block_positions(view, p, n):
    if p == 0:
        return view[:, n * P:(n + 1) * P]
    if p == 1:
        start = n // 2 + 512 * (n % 2)
        return view[:, start:start + 4 * (P - 1) + 1:4]
    return view[:, n:n + 8 * (P - 1) + 1:8]


def trunk(nc, x, positions, gains, sinks_0, final_norm, w_qkv, w_gate, w_out, out):
    ctx = ExitStack()
    with ctx:
        def sb(name, shape, dt=F32):
            return ctx.enter_context(nc.sbuf_tensor(name, shape, dt))

        def sem(name):
            return ctx.enter_context(nc.semaphore(name))

        def bank(name):
            return ctx.enter_context(nc.psum_tensor(name, [P, 512], F32))

        ht = [sb("ht_hi", [P, KT, S], F32R), sb("ht_lo", [P, KT, S], F32R)]
        w_raw = sb("w_raw", [P, 2, 2, QKV])
        w_split = [sb("w_hi", [P, 3, 4, QKV], F32R), sb("w_lo", [P, 3, 4, QKV], F32R)]
        qk = sb("qk", [P, NB, R * HD + 2 * HD])
        v = sb("v", [P, 2, NB, HD])
        qs = sb("qs", [P, R, S], F32R)
        ks = sb("ks", [P, 2, S], F32R)
        probs = sb("probs", [P, PROBS, 2, 2, P])
        probs_t = sb("probs_t", [P, 2, 4, P])
        xr = sb("xr", [P, NB, D])
        ot = [xr[:, 2 * i:2 * i + 2, :] for i in range(4)]
        gate = sb("gate", [P, 2, S])
        coef = sb("coef", [P, 2, 512])
        masks = sb("masks", [P, 4, P])
        ident = sb("ident", [P, P])
        stat = sb("stat", [P, 2, NB, 2 * R])
        nat = sb("nat", [P, 3, NB, 2 * R])
        comb = sb("comb", [P, 2, 3, NB, R])
        comb_small = sb("comb_small", [P, 2, NB, R])
        coef_rows = sb("coef_rows", [3 * NB * R, P])
        mx = sb("mx", [P, 2, 2])
        sink = sb("sink", [P, H])
        neg_sink = sb("neg_sink", [P, H])
        no_sink = sb("no_sink", [P, 2])
        pos_i = sb("pos_i", [P, 3, NB], I32)
        pos_f = sb("pos_f", [P, 3, NB])
        rope_w = gate[:, 0, 0:9 * NB * HALF_ROT].rearrange("p (a b) -> p a b", a=3)
        cosines = sb("cosines", [P, 3, NB, ROT])
        sines = sb("sines", [P, 3, NB, ROT])
        rot = sb("rot", [P, 2, 6, ROT])
        gain = sb("gain", [P, 2, KT])
        ssq = sb("ssq", [P, 4, NB])
        sums = sb("sums", [P, NB])

        s_bank = [bank(f"s_bank{i}") for i in range(2)]
        t_bank = [bank(f"t_bank{i}") for i in range(2)]
        o_bank = [bank(f"o_bank{i}") for i in range(2)]
        j_bank = [bank(f"j_bank{i}") for i in range(2)]

        def dram(name, shape):
            return nc.dram_tensor(name, shape, F32).ap()

        mix_dram = dram("mix_dram", [2, D, S])
        x1_dram = dram("x1_dram", [S, D])
        stat_dram = dram("stat_dram", [GROUPS * 3, S, 2 * R])
        coef_dram = dram("coef_dram", [2 * GROUPS, 3, NB, R, P])

        x2d = x.rearrange("a s d -> (a s) d")
        out2d = out.rearrange("a s d -> (a s) d")
        packed = {"qkv": w_qkv, "gate": w_gate, "out": w_out}
        qk_flat = qk[:, :, :].rearrange("p a b -> p (a b)")
        res = [qk_flat[:, 0:NB * OUT_COLS].rearrange("p (a c) -> p a c", c=OUT_COLS),
               gate[:, :, :].rearrange("p a (b c) -> p (a b) c", c=OUT_COLS)]
        mix_in = [qk_flat[:, i * S:(i + 1) * S] for i in range(3)]
        square_a = probs_t[:, :, :, :].rearrange("p a b c -> p (a b c)")
        square_v = probs[:, :, :, :, :].rearrange("p a b c d -> p (a b c d)")[:, 0:D]
        gain_row = coef[:, :, :].rearrange("p a b -> p (a b)")

        parity = gate[:, 1, 0:P].bitcast(I32)
        spare = {2: s_bank[0], 3: s_bank[1], 4: o_bank[0], 5: o_bank[1]}
        norm_bank = [s_bank[0], s_bank[1], o_bank[0], o_bank[1]]

        def gate_of(layer, g):
            return ot[0] if layer == 0 and g == GROUPS - 1 else gate

        def weights(job, part, kt):
            return w_split[part][:, half_slot(JOB[job], kt // 4), kt % 4, 0:columns(job)]

        def quarter(n, q, part):
            return w_split[part][:, half_slot(n, q // 2), 2 * (q % 2):2 * (q % 2) + 2, 0:columns(JOBS[n])]

        def raw_quarter(n, q):
            return w_raw[:, q % 2, :, 0:columns(JOBS[n])]

        x_in = [sem(f"x_in{i}") for i in range(NB)]
        small_in = sem("small_in")
        raw_in = [sem(f"raw_in{i}") for i in range(2)]
        mix_back = [sem(f"mix_back{i}") for i in range(3)]
        res_in = [sem(f"res_in{i}") for i in range(2)]
        nat_in = sem("nat_in")
        coef_in = [sem(f"coef_in{i}") for i in range(2)]
        gain_in = sem("gain_in")
        stat_out = [sem(f"stat_out{i}") for i in range(2)]
        coef_out = sem("coef_out")
        mix_out = sem("mix_out")
        x1_out = sem("x1_out")
        x1_last_out = [sem(f"x1_last_out{i}") for i in range(2)]
        final_out = sem("final_out")
        piece_full = sem("piece_full")
        spare_full = sem("spare_full")
        norm_full = sem("norm_full")
        turned = sem("turned")
        job_done = sem("job_done")
        scored = sem("scored")
        summed = sem("summed")
        piece_empty = {"a": sem("piece_empty_a"), "v": sem("piece_empty_v")}
        turn_empty = {"a": sem("turn_empty_a"), "v": sem("turn_empty_v")}
        spare_empty = sem("spare_empty")
        norm_empty = {"a": sem("norm_empty_a"), "v": sem("norm_empty_v")}
        masked = sem("masked")
        biased = sem("biased")
        exped = sem("exped")
        w_hi_done = sem("w_hi_done")
        w_lo_done = {"v": sem("w_lo_v"), "p": sem("w_lo_p")}
        ot_stored = sem("ot_stored")
        silued = sem("silued")
        den_v = sem("den_v")
        den_a = sem("den_a")
        mixed = sem("mixed")
        mix_hi = sem("mix_hi")
        mix_lo = sem("mix_lo")
        squared = {"a": sem("squared_a"), "v": sem("squared_v")}
        norm_v = sem("norm_v")
        norm_a = sem("norm_a")
        xn_done = {"a": sem("xn_a"), "v": sem("xn_v")}
        final_done = sem("final_done")
        rope_v = sem("rope_v")
        rope_a = sem("rope_a")
        tables = sem("tables")
        sink_neg = sem("sink_neg")
        mask_v = sem("mask_v")
        norm_r = sem("norm_r")
        rotated = sem("rotated")
        rot_link = sem("rot_link")
        consts = sem("consts")
        const_link = sem("const_link")

        block = ctx.enter_context(nc.Block())

        def wait_piece_emptied(eng, key, by="av"):
            for e in by:
                if e in PIECE.uses[PIECE.at[key]]:
                    eng.wait_ge(piece_empty[e], PIECE.emptied(key, e))

        def wait_turn_emptied(eng, key):
            for e in TURN.uses[TURN.at[key]]:
                eng.wait_ge(turn_empty[e], TURN.emptied(key, e))

        def links_per_group(layer):
            return 4 if layer == 0 else 7

        def links_before(t):
            return sum(links_per_group(s.layer) for s in STEPS[:t] if s.ends_group)

        def groups_before(t):
            return sum(s.ends_group for s in STEPS[:t])

        def mix_links(s):
            return sum(1 + (p > 0) for _, _, p in mix_items(s)) + 4

        def mix_links_before(t):
            return sum(mix_links(s) for s in STEPS[:t] if s.ends_group)

        def coef_loads_before(t):
            return sum(len(mix_items(s)) for s in STEPS[:t] if s.ends_group)

        def out_region(s):
            return (s.t - s.p) % 4

        MIX_LOADS = 2 * (GROUPS - 1)
        MIX_TILES = MIX_LOADS + 2

        def stat_stored(t):
            return 16 * sum(2 if s.p == 1 else 1 for s in STEPS[GROUPS:t + 1] if s.t % 2 == t % 2)

        def product_link(index):
            seen = 0
            for s in STEPS:
                if s.ends_group:
                    done = mix_links_before(s.t)
                    for k, (r, half, p) in enumerate(mix_items(s)):
                        done += 1
                        if seen == index:
                            return done
                        seen += 1
                        if p > 0:
                            done += 1
                        if k + 1 == len(mix_items(s)) or mix_items(s)[k + 1][2] == 0:
                            done += 1
            raise ValueError(index)

        NORM_LINKS = 6
        ROPE_LINKS = 26

        def row_ready(k):
            def wait(eng, n):
                if k == 0:
                    eng.wait_ge(x_in[n], 16)
                else:
                    eng.wait_ge(piece_empty["v"], PIECE.emptied(("out", k - 1, OUT_JOBS - 1, n), "v"))
            return wait

        def splits_of(phase, *where):
            if phase == "start":
                return [(0, 0), (0, 1)]
            if phase == "start, later":
                return [(0, 2), (0, 3), (1, 0), (1, 1)]
            layer, c = where
            n = JOB[("out", layer, c)]
            if phase == "job":
                return [(n, 2), (n, 3)] if c > 0 else []
            if phase == "mid-job":
                return [(n + 1, 0), (n + 1, 1)] if n + 1 < len(JOBS) else []
            return [(n + 1, 2), (n + 1, 3), (n + 2, 0), (n + 2, 1)]

        def guard_qkv(eng, key):
            _, t, k = key
            s = STEPS[t]
            if not s.first:
                eng.wait_ge(turned, TURN.filled((t - 1, "Q1", k // 4)))
            elif t > 0:
                eng.wait_ge(piece_empty["v"], PIECE.emptied(("out", 0, OUT_JOBS - 2, NB - 1), "v"))
            if t >= 2:
                eng.wait_ge(summed, UNITS * (t - 1))

        def guard_gate(eng, key):
            _, layer, g, k = key
            t = [s.t for s in STEPS if s.layer == layer and s.g == g and s.ends_group][0]
            if layer == 0 and g == GROUPS - 1:
                eng.wait_ge(mix_out, 32)
            elif t > 0 and g > 0:
                eng.wait_ge(mixed, mix_links_before(t))
            elif layer == 1:
                eng.wait_ge(piece_empty["v"], PIECE.emptied(("out", 0, OUT_JOBS - 1, NB - 1), "v"))

        def guard_fill(eng, t, what, half):
            s = STEPS[t]
            if not s.first:
                last = 8 + 4 * half + 4 if what == "K" else 8 * int(what[1]) + 4 * half + 4
                if what == "K":
                    last = 13 if half == 0 else UNITS
                eng.wait_ge(scored, UNITS * (t - 1) + last)

        def guard_scale(eng, layer, half):
            if layer == 1:
                eng.wait_ge(x1_out, 16 * (OUT_JOBS - 1))
                eng.wait_ge(x1_last_out[half], 16)

        def store_turn(eng, copy, s, u):
            r, n = u // NB, u % NB
            i = UNITS * s.t + u
            key = (s.t, u)
            eng.wait_ge(turned, TURN.filled(key))
            if i >= 2:
                eng.wait_ge(summed, i - 1)
            src = t_bank[TURN.bank(key)][:, :].rearrange("p (j e q) -> p j e q", j=2, e=2)
            to = probs_t[:, i % 2, :, :].rearrange("p (j e) q -> p j e q", e=2)
            lo = 0 if s.has_prev(n) else 1
            return copy(to[:, :, lo:2, :], src[:, :, lo:2, :])

        @block.sync
        def _(sp):
            def raw(n, q):
                m = 4 * n + q
                if n >= len(JOBS):
                    return
                job = JOBS[n]
                if m >= 2:
                    sp.wait_ge(w_lo_done["vp"[q % 2]], m // 2)
                src = packed[job[0]][packed_index(job)].rearrange("p (k c) -> p k c", k=KT)
                sp.dma_start(raw_quarter(n, q), src[:, 2 * q:2 * q + 2, :]).then_inc(raw_in[q % 2], 16)

            def raws_after(quarters):
                for n, q in quarters:
                    raw(n + q // 2, (q + 2) % 4)

            def stats_out(s):
                sp.wait_ge(exped, UNITS * (s.t + 1))
                n = s.t - GROUPS
                src = stat[:, s.t % 2, :, :]
                if s.p == 0:
                    sp.dma_start(stat_dram[n].rearrange("(n i) c -> i n c", n=NB), src).then_inc(stat_out[s.t % 2], 16)
                elif s.p == 1:
                    to = stat_dram[n].rearrange("(b i f) c -> i b f c", b=2, f=4)
                    for b in range(2):
                        sp.dma_start(to[:, b, :, :], src[:, b:NB:2, :]).then_inc(stat_out[s.t % 2], 16)
                else:
                    sp.dma_start(stat_dram[n].rearrange("(i n) c -> i n c", n=NB), src).then_inc(stat_out[s.t % 2], 16)

            def stats_in(s):
                for q in (s.t - 1, s.t):
                    sp.wait_ge(stat_out[q % 2], stat_stored(q))
                if s.g > 0:
                    sp.wait_ge(den_v, links_before(s.t))
                for p in range(3):
                    sp.dma_start(nat[:, p, :, :], stat_dram[3 * s.g + p].rearrange("(n i) c -> i n c", n=NB)).then_inc(nat_in, 16)

            def coef_store(s):
                n = groups_before(s.t)
                rows = (1 if s.layer == 0 else 3) * NB * R
                sp.wait_ge(turn_empty["v"], TURN.emptied(("C", s.t), "v"))
                to = coef_dram[n].rearrange("p n h i -> (p n h) i")
                sp.dma_start(to[0:rows, :], coef_rows[0:rows, :]).then_inc(coef_out, 16)

            def coef_load(s, k):
                n = groups_before(s.t)
                r, half, p = mix_items(s)[k]
                index = coef_loads_before(s.t) + k
                buf = index % 2
                sp.wait_ge(coef_out, 16 * (n + 1))
                if index >= 2:
                    sp.wait_ge(mixed, product_link(index - 2))
                for j in range(2):
                    src = coef_dram[n, p, 4 * half:4 * half + 4, 2 * r + j, :]
                    src = src.rearrange("(o n) i -> o n i", o=1).broadcast_to([HD, 4, P])
                    sp.dma_start(coef[64 * j:64 * j + 64, buf, :].rearrange("p (n i) -> p n i", n=4), src).then_inc(coef_in[buf], 16)

            def mix_store(s):
                sp.wait_ge(mixed, mix_links_before(s.t) + mix_links(s))
                for r in range(2):
                    row = (2 * s.g + r) * P
                    sp.dma_start(mix_dram[s.layer, row:row + P, :], ot[out_region(s)][:, r, :]).then_inc(mix_out, 16)

            def mix_load(layer, k):
                last = LAYER_STEPS[layer][-1]
                n = layer * MIX_LOADS + k
                sp.wait_ge(mix_out, 32 * ((GROUPS - 1) * layer + k // 2 + 1))
                if k < 3:
                    sp.wait_ge(turned, TURN.filled((last.t, "Q1", 1)))
                else:
                    sp.wait_ge(mix_lo, layer * MIX_TILES + k - 2)
                sp.dma_start(mix_in[k % 3], mix_dram[layer, k * P:(k + 1) * P, :]).then_inc(mix_back[n % 3], 16)

            def res_load(layer, c):
                if c == 0:
                    sp.wait_ge(mix_lo, layer * MIX_TILES + MIX_LOADS)
                elif c == 1:
                    sp.wait_ge(mixed, mix_links_before(STEPS[-1].t + 1 if layer else GROUPS))
                else:
                    sp.wait_ge(piece_empty["v"], PIECE.emptied(("out", layer, c - 2, NB - 1), "v"))
                if layer == 1 and c == 0:
                    sp.wait_ge(x1_out, 16 * (OUT_JOBS - 1))
                    for half in range(2):
                        sp.wait_ge(x1_last_out[half], 16)
                src = (x2d, x1_dram)[layer]
                sp.dma_start(res[c % 2], src.rearrange("(n i) d -> i n d", n=NB)[:, :, c * OUT_COLS:(c + 1) * OUT_COLS]).then_inc(res_in[c % 2], 16)

            def x1_store(c, rows, done):
                sp.wait_ge(piece_empty["v"], PIECE.emptied(("out", 0, c, rows[-1]), "v"))
                cols = slice(c * OUT_COLS, (c + 1) * OUT_COLS)
                blocks = slice(rows[0], rows[-1] + 1)
                sp.dma_start(x1_dram.rearrange("(n i) d -> i n d", n=NB)[:, blocks, cols], xr[:, blocks, cols]).then_inc(done, 16)

            def out_rows(blocks):
                for n in blocks:
                    sp.wait_ge(final_done, n + 1)
                    sp.dma_start(out2d[n * P:(n + 1) * P, :], xr[:, n, :]).then_inc(final_out, 16)

            sp.dma_start(gain[:, :, :], gains).then_inc(small_in, 16)
            for n in range(NB):
                if n == 4:
                    raw(0, 0)
                    raw(0, 1)
                sp.dma_start(xr[:, n, :], x2d[n * P:(n + 1) * P, :]).then_inc(x_in[n], 16)
            sp.dma_start(sink[:, :], sinks_0.rearrange("(o h) -> o h", o=1).broadcast_to([P, H])).then_inc(small_in, 16)
            sp.dma_start(pos_i[:, :, :], positions).then_inc(small_in, 16)
            raws_after(splits_of("start") + splits_of("start, later"))
            for layer in (0, 1):
                steps = LAYER_STEPS[layer]
                for s in steps:
                    before = None if s.first else STEPS[s.t - 1]
                    for slot in range(UNITS):
                        raws_after(SLOT_SPLIT.get((s.t, slot), []))
                        if before is not None:
                            if slot == 1 and layer == 1:
                                stats_out(before)
                                if before.ends_group:
                                    stats_in(before)
                            if before.ends_group:
                                items = range(len(mix_items(before)))
                                if slot == LATE_C:
                                    coef_store(before)
                                    coef_load(before, 0)
                                    coef_load(before, 1)
                                for k in items:
                                    if mix_slot(before, k) == slot and k + 2 in items:
                                        coef_load(before, k + 2)
                                if slot == mix_slot(before, items[-1]) + 1:
                                    mix_store(before)
                        if s.last:
                            if slot == 4:
                                for k in range(3):
                                    mix_load(layer, k)
                            for k in range(3, MIX_LOADS):
                                if slot == max(SPLIT_MIX[k - 3] + 1, 12 if k > 3 else 0):
                                    mix_load(layer, k)
                last = steps[-1]
                if layer == 1:
                    stats_out(last)
                    stats_in(last)
                coef_store(last)
                coef_load(last, 0)
                coef_load(last, 1)
                res_load(layer, 0)
                for k in range(2, len(mix_items(last))):
                    coef_load(last, k)
                res_load(layer, 1)
                if layer == 1:
                    sp.wait_ge(mixed, mix_links_before(last.t) + mix_links(last))
                    sp.dma_start(gain_row, final_norm.rearrange("(o d) -> o d", o=1).broadcast_to([P, D])).then_inc(gain_in, 16)
                for c in range(OUT_JOBS):
                    raws_after(splits_of("job", layer, c) + splits_of("mid-job", layer, c))
                    if c + 1 < OUT_JOBS:
                        if layer == 0:
                            x1_store(c, range(NB), x1_out)
                        if c + 2 < OUT_JOBS:
                            res_load(layer, c + 2)
                if layer == 0:
                    for half in range(2):
                        x1_store(OUT_JOBS - 1, range(4 * half, 4 * half + 4), x1_last_out[half])
                    raws_after(splits_of("next", layer, OUT_JOBS - 1))
            out_rows(range(NB))
            sp.wait_ge(final_out, 16 * NB)

        @block.gpsimd
        def _(pool):
            pool.memset(ident[:, :], 0.0).then_inc(const_link, 1)
            pool.memset(masks[:, :, :], 0.0).then_inc(const_link, 1)
            pool.memset(no_sink[:, :], BIG).then_inc(const_link, 1)
            pool.wait_ge(const_link, 2)
            pool.affine_select(out=ident[:, :], in_=ident[:, :], compare_op=ALU.not_equal, fill=1.0, base=0,
                               pattern=[[-1, P]], channel_multiplier=1).then_inc(const_link, 1)
            for m in (2, 3):
                own = masks[:, m, :]
                pool.affine_select(out=own, in_=own, compare_op=ALU.is_ge, fill=MASKED, base=0,
                                   pattern=[[-1, P]], channel_multiplier=1).then_inc(const_link, 1)
            for m in (0, 1):
                prev = masks[:, m, :]
                pool.affine_select(out=prev, in_=prev, compare_op=ALU.is_ge, fill=MASKED, base=-m,
                                   pattern=[[1, P]], channel_multiplier=-1).then_inc(const_link, 1)
            pool.iota(parity[:, :], pattern=[[1, P]], base=0, channel_multiplier=1).then_inc(const_link, 1)
            pool.wait_ge(const_link, 9)
            pool.sem_inc(consts, 1)

            def w_lo(quarters):
                for n, q in quarters:
                    if q % 2 == 1:
                        pool.wait_ge(w_hi_done, 4 * n + q + 1)
                        pool.tensor_tensor(quarter(n, q, 1), raw_quarter(n, q), quarter(n, q, 0).bitcast(F32),
                                           ALU.subtract).then_inc(w_lo_done["p"], 1)

            def rotate(t, half):
                p = STEPS[t].p
                for k in (4 * half + 2, 4 * half + 3):
                    wait_piece_emptied(pool, ("qkv", t, k))
                if t == 0 and half == 0:
                    pool.wait_ge(tables, 1)
                for i in range(2):
                    base = 4 * (4 * t + 2 * half + i)
                    if base > 0:
                        pool.wait_ge(rot_link, base)
                    rows = slice(4 * half + 2 * i, 4 * half + 2 * i + 2)
                    xs = qk[:, rows, :].rearrange("p n (h c) -> p n h c", c=HD)
                    cos = cosines[:, p, rows, :].rearrange("p n (o c) -> p n o c", o=1).broadcast_to([P, 2, 6, ROT])
                    sin = sines[:, p, rows, :].rearrange("p n (o c) -> p n o c", o=1).broadcast_to([P, 2, 6, ROT])
                    lower, upper = slice(0, HALF_ROT), slice(HALF_ROT, ROT)
                    pool.tensor_tensor(rot[:, :, :, lower], xs[:, :, :, upper], sin[:, :, :, lower], ALU.mult).then_inc(rot_link, 1)
                    pool.tensor_tensor(rot[:, :, :, upper], xs[:, :, :, lower], sin[:, :, :, upper], ALU.mult).then_inc(rot_link, 1)
                    pool.wait_ge(rot_link, base + 2)
                    pool.tensor_tensor(xs[:, :, :, 0:ROT], xs[:, :, :, 0:ROT], cos, ALU.mult).then_inc(rot_link, 1)
                    pool.wait_ge(rot_link, base + 3)
                    last = pool.tensor_tensor(xs[:, :, :, 0:ROT], xs[:, :, :, 0:ROT], rot[:, :, :, :], ALU.add).then_inc(rot_link, 1)
                pool.wait_ge(rot_link, base + 4)
                pool.sem_inc(rotated, 1)

            w_lo(splits_of("start") + splits_of("start, later"))
            for layer in (0, 1):
                steps = LAYER_STEPS[layer]
                for half in range(2):
                    rotate(steps[0].t, half)
                for s in steps:
                    pieces = [slot for slot in range(UNITS) for x_ in SLOT_PIECES.get((s.t, slot), []) if x_[0] == "qkv"]
                    for slot in range(UNITS):
                        w_lo(SLOT_SPLIT.get((s.t, slot), []))
                        if not s.last and slot == pieces[3] + 1:
                            rotate(s.t + 1, 0)
                        if not s.last and slot == pieces[7] + 1:
                            rotate(s.t + 1, 1)
                for c in range(OUT_JOBS):
                    w_lo(splits_of("job", layer, c) + splits_of("mid-job", layer, c))
                if layer == 0:
                    w_lo(splits_of("next", layer, OUT_JOBS - 1))

        @block.tensor
        def _(pe):
            def free_bank(ring, empty, key):
                for e, count in ring.free(key):
                    pe.wait_ge(empty[e], count)

            def norm_piece(layer, kt, half):
                i = KT * half + kt
                if i >= 4:
                    pe.wait_ge(norm_empty["v"], 2 * KT * layer + i - 3)
                elif layer == 1:
                    pe.wait_ge(spare_empty, len(SPARE))
                if kt == 0:
                    for e in "av":
                        pe.wait_ge(xn_done[e], 4 * layer + 2 * half + 2)
                for b in range(4):
                    last = pe.transpose(norm_bank[i % 4][:, b * P:(b + 1) * P],
                                        xr[:, 4 * half + b, kt * P:(kt + 1) * P], ident[:, :])
                last.then_inc(norm_full, 1)

            def products(to, a, b, kts, start, stop):
                for kt in kts:
                    for x_, y_ in ((0, 0), (0, 1), (1, 0)):
                        last = pe.matmul(to, a(x_, kt), b(y_, kt), start=(start and kt == kts[0] and x_ == y_),
                                         stop=(stop and kt == kts[-1] and x_ == 1))
                return last

            def weights_half(job, half):
                for e in "vp":
                    pe.wait_ge(w_lo_done[e], 2 * JOB[job] + half + 1)

            def operands(job, k):
                if job[0] == "gate":
                    r, half = k // 2, k % 2
                    return (lambda i, kt: weights(job, i, kt)[:, r * P:(r + 1) * P],
                            lambda i, kt: ht[i][:, kt, half * 512:(half + 1) * 512], 512)
                p = STEPS[job[1]].p if job[0] == "qkv" else 0
                return (lambda i, kt: block_positions(ht[i][:, kt, :], p, k),
                        lambda i, kt: weights(job, i, kt), columns(job))

            def piece(key):
                job, k = key[:-1], key[-1]
                free_bank(PIECE, piece_empty, key)
                if job[0] == "qkv" and STEPS[job[1]].first:
                    for e in "av":
                        pe.wait_ge(norm_empty[e], 2 * KT * STEPS[job[1]].layer + KT * (k // 4 + 1))
                a, b, cols = operands(job, k)
                to = j_bank[PIECE.bank(key)][:, 0:cols]
                for half in range(2):
                    if k == 0:
                        weights_half(job, half)
                    last = products(to, a, b, range(4 * half, 4 * half + 4), half == 0, half == 1)
                last.then_inc(piece_full, 1)
                if k == (4 if job[0] == "gate" else NB) - 1:
                    pe.wait_ge(piece_full, PIECE.filled(key))
                    pe.sem_inc(job_done, 1)

            def out_bank(layer, k):
                return (spare[k] if k in SPARE else j_bank[PIECE.bank(("out", layer, 0, k))])[:, 0:OUT_COLS]

            def early_row(layer, k):
                job = ("out", layer, 0)
                last_step = LAYER_STEPS[layer][-1]
                if k == 0:
                    for half in range(2):
                        weights_half(job, half)
                    pe.wait_ge(mix_lo, layer * MIX_TILES + MIX_LOADS)
                    pe.wait_ge(mix_hi, layer * MIX_TILES + MIX_LOADS)
                if k not in SPARE:
                    free_bank(PIECE, piece_empty, job + (k,))
                elif k < 4:
                    pe.wait_ge(biased, UNITS * (last_step.t + 1))
                else:
                    pe.wait_ge(ot_stored, 4 * (last_step.t + 1))
                a, b, _ = operands(job, k)
                products(out_bank(layer, k), a, b, range(MIX_LOADS), True, False)

            def late_row(layer, k):
                job = ("out", layer, 0)
                if k == 0:
                    pe.wait_ge(mix_lo, (layer + 1) * MIX_TILES)
                    pe.wait_ge(mix_hi, (layer + 1) * MIX_TILES)
                a, b, _ = operands(job, k)
                last = products(out_bank(layer, k), a, b, range(MIX_LOADS, KT), False, True)
                last.then_inc(spare_full if k in SPARE else piece_full, 1)

            def fill(t, what, half):
                key = (t, what, half)
                free_bank(TURN, turn_empty, key)
                pe.wait_ge(rotated, 2 * t + half + 1)
                c0 = R * HD if what == "K" else int(what[1]) * P
                for i in range(4):
                    last = pe.transpose(t_bank[TURN.bank(key)][:, i * P:(i + 1) * P],
                                        qk[:, 4 * half + i, c0:c0 + P], ident[:, :])
                last.then_inc(turned, 1)

            def score(s, u):
                r, n = u // NB, u % NB
                i = UNITS * s.t + u
                if s.first and u == 0:
                    pe.wait_ge(norm_empty["v"], 2 * KT * (s.layer + 1))
                if i >= 2:
                    pe.wait_ge(biased, i - 1)
                if n % 4 == 0:
                    wait_turn_emptied(pe, (s.t, "K", n // 4))
                    wait_turn_emptied(pe, (s.t, f"Q{r}", n // 4))
                lo = 0 if s.has_prev(n) else P
                for j in range(2):
                    to = s_bank[i % 2][:, 2 * P * j + lo:2 * P * (j + 1)]
                    for part in range(2):
                        last = pe.matmul(to, qs[:, 2 * r + j, n * P:(n + 1) * P],
                                         ks[:, part, (n - 1) * P + lo:(n + 1) * P], start=(part == 0), stop=(part == 1))
                last.then_inc(scored, 1)

            def turn(s, u):
                r, n = u // NB, u % NB
                i = UNITS * s.t + u
                key = (s.t, u)
                free_bank(TURN, turn_empty, key)
                pe.wait_ge(exped, i + 1)
                for j in range(2):
                    for side in range(0 if s.has_prev(n) else 1, 2):
                        last = pe.transpose(t_bank[TURN.bank(key)][:, (2 * j + side) * P:(2 * j + side + 1) * P],
                                            probs[:, i % PROBS, j, side, :], ident[:, :])
                last.then_inc(turned, 1)

            def times_v(s, u):
                r, n = u // NB, u % NB
                i = UNITS * s.t + u
                group = 4 * s.t + 2 * r + n // 4
                wait_turn_emptied(pe, (s.t, u))
                if n % 4 == 0:
                    if group >= 2:
                        pe.wait_ge(ot_stored, group - 1)
                if u == 0 or u == 4:
                    for k in (4 * (u // 4) + 2, 4 * (u // 4) + 3):
                        wait_piece_emptied(pe, ("qkv", s.t, k))
                sides = [0, 1] if s.has_prev(n) else [1]
                for side in sides:
                    for j in range(2):
                        last = pe.matmul(o_bank[group % 2][64 * j:64 * j + 64, (n % 4) * P:(n % 4 + 1) * P],
                                         v[:, s.t % 2, n - 1 + side, :], probs_t[:, i % 2, 2 * j + side, :],
                                         start=(side == sides[0]), stop=(side == 1))
                last.then_inc(summed, 1)

            def coef_turn(s):
                key = ("C", s.t)
                rows = (1 if s.layer == 0 else 3) * NB * R
                free_bank(TURN, turn_empty, key)
                pe.wait_ge(den_v, links_before(s.t) + links_per_group(s.layer))
                src = comb[:, 1 - s.layer, :, :, :].rearrange("p a b c -> p (a b c)")[:, 0:rows]
                pe.transpose(t_bank[TURN.bank(key)][0:rows, 0:P], src, ident[:, :]).then_inc(turned, 1)

            pe.wait_ge(consts, 1)
            for kt in range(KT):
                norm_piece(0, kt, 0)
            for layer in (0, 1):
                steps = LAYER_STEPS[layer]
                for k in range(NB):
                    piece(("qkv", steps[0].t, k))
                    if k < 4:
                        for kt in (2 * k, 2 * k + 1):
                            norm_piece(layer, kt, 1)
                for what, half in FILLS_BEFORE.values():
                    fill(steps[0].t, what, half)
                for s in steps:
                    for slot in range(UNITS):
                        score(s, slot)
                        for key in SLOT_PIECES.get((s.t, slot), []):
                            piece(key)
                        b, u = unit_before(s, slot, 1)
                        if b:
                            turn(b, u)
                        if slot in FILLS_WITHIN:
                            fill(s.t, *FILLS_WITHIN[slot])
                        if slot in FILLS_BEFORE and not s.last:
                            fill(s.t + 1, *FILLS_BEFORE[slot])
                        if slot == LATE_C and not s.first and STEPS[s.t - 1].ends_group:
                            coef_turn(STEPS[s.t - 1])
                        b, u = unit_before(s, slot, 2)
                        if b:
                            times_v(b, u)
                last = steps[-1]
                turn(last, UNITS - 1)
                times_v(last, UNITS - 2)
                times_v(last, UNITS - 1)
                for k in range(EARLY):
                    early_row(layer, k)
                    if k == 2:
                        coef_turn(last)
                for k in range(EARLY):
                    late_row(layer, k)
                for c in range(OUT_JOBS):
                    for k in range(EARLY if c == 0 else 0, NB):
                        piece(("out", layer, c, k))
                        if layer == 0 and c == OUT_JOBS - 1 and k >= 6:
                            for kt in range(4 * (k - 6), 4 * (k - 6) + 4):
                                norm_piece(1, kt, 0)

        @block.scalar
        def _(act):
            def w_hi(quarters):
                for n, q in quarters:
                    act.wait_ge(raw_in[q % 2], 16 * ((4 * n + q) // 2 + 1))
                    if n >= 2 or (n == 1 and q >= 2):
                        act.wait_ge(job_done, n - 1 + q // 2)
                    act.activation(quarter(n, q, 0), raw_quarter(n, q), ACT.Copy).then_inc(w_hi_done, 1)

            def exps(s, u):
                r, n = u // NB, u % NB
                i = UNITS * s.t + u
                lo = 0 if s.has_prev(n) else P
                act.wait_ge(biased, i + 1)
                for j in range(2):
                    h = 2 * r + j
                    row = probs[:, i % PROBS, j, lo // P:2, :]
                    last = act.activation(row, row, ACT.Exp, bias=stat[:, s.t % 2, n, h:h + 1], scale=SCALE,
                                          accum_out=stat[:, s.t % 2, n, R + h:R + h + 1])
                last.then_inc(exped, 1)

            def empty_piece(key):
                if "a" not in PIECE.uses[PIECE.at[key]]:
                    return
                act.wait_ge(piece_full, PIECE.filled(key))
                src = j_bank[PIECE.bank(key)]
                if key[0] == "qkv":
                    k = key[2]
                    guard_qkv(act, key)
                    act.activation(qk[:, k, 0:R * HD + HD], src[:, 0:R * HD + HD], ACT.Copy)
                    act.activation(qk[:, k, R * HD + HD:], src[:, R * HD:R * HD + HD], ACT.Copy)
                    last = act.activation(v[:, key[1] % 2, k, :], src[:, R * HD + HD:QKV], ACT.Copy)
                elif key[0] == "gate":
                    r, half = key[3] // 2, key[3] % 2
                    guard_gate(act, key)
                    last = act.activation(gate_of(key[1], key[2])[:, r, half * 512:(half + 1) * 512], src[:, :], ACT.Copy)
                last.then_inc(piece_empty["a"], 1)

            def empty_norm(layer, kt, half):
                i = KT * half + kt
                act.wait_ge(norm_full, 2 * KT * layer + i + 1)
                if layer == 0 and i == 0:
                    act.wait_ge(small_in, 48)
                if layer == 1 and kt == 0:
                    act.wait_ge(piece_full, PIECE.filled(("out", 0, OUT_JOBS - 1, 4 * half + 3)))
                act.activation(ht[0][:, kt, half * 512:(half + 1) * 512], norm_bank[i % 4][:, :], ACT.Copy,
                               scale=gain[:, layer, kt:kt + 1]).then_inc(norm_empty["a"], 1)

            def empty_turn(s, u):
                if u % 2 == 0:
                    store_turn(act, act.copy, s, u).then_inc(turn_empty["a"], 1)

            def fill_hi(t, what, half):
                key = (t, what, half)
                act.wait_ge(turned, TURN.filled(key))
                guard_fill(act, t, what, half)
                src = t_bank[TURN.bank(key)]
                cols = slice(half * 512, (half + 1) * 512)
                if what == "K":
                    last = act.activation(ks[:, 0, cols], src[:, :], ACT.Copy)
                else:
                    h = 2 * int(what[1])
                    act.activation(qs[0:64, h, cols], src[0:64, :], ACT.Copy)
                    last = act.activation(qs[64:P, h + 1, cols], src[64:P, :], ACT.Copy)
                last.then_inc(turn_empty["a"], 1)

            def silu(s):
                for k in range(4):
                    wait_piece_emptied(act, ("gate", s.layer, s.g, k))
                tile = gate_of(s.layer, s.g)[:, :, :]
                act.activation(tile, tile, ACT.Silu).then_inc(silued, 1)

            def den_exp(s):
                n = links_before(s.t)
                if s.layer == 0:
                    act.wait_ge(den_v, n + 1)
                    e = comb[:, 0, 0, :, :]
                else:
                    act.wait_ge(den_v, n + 3)
                    e = comb[:, 0, :, :, :]
                act.activation(e, e, ACT.Exp).then_inc(den_a, 1)

            def mix_split(layer, k, src):
                act.activation(ht[0][:, k, :], src, ACT.Copy).then_inc(mix_hi, 1)

            def square(k, n):
                row_ready(k)(act, n)
                count = 4 * k + n // 2
                if count > 0:
                    act.wait_ge(squared["a"], count)
                act.activation(square_a, xr[:, n, :], ACT.Square, accum_out=sums[:, n:n + 1]).then_inc(squared["a"], 1)

            def root(k, half):
                act.wait_ge(norm_v, NORM_LINKS * (2 * k + half) + 1)
                blocks = slice(4 * half, 4 * half + 4)
                act.activation(ssq[:, 1, blocks], ssq[:, 0, blocks], ACT.Sqrt).then_inc(norm_a, 1)

            def scale_rows(layer, half):
                act.wait_ge(norm_v, NORM_LINKS * (2 * layer + half + 1))
                guard_scale(act, layer, half)
                for n in (4 * half, 4 * half + 2):
                    act.activation(xr[:, n, :], xr[:, n, :], ACT.Copy, scale=ssq[:, 2, n:n + 1]).then_inc(xn_done["a"], 1)

            def norm_half(layer, half):
                square(layer, 4 * half)
                square(layer, 4 * half + 2)
                root(layer, half)
                scale_rows(layer, half)

            norm_half(0, 0)
            w_hi(splits_of("start"))
            for kt in range(KT):
                empty_norm(0, kt, 0)
            norm_half(0, 1)
            w_hi(splits_of("start, later"))
            for layer in (0, 1):
                steps = LAYER_STEPS[layer]
                for k in range(NB):
                    if layer == 0 and k == 4:
                        act.wait_ge(rope_v, ROPE_LINKS)
                        act.activation(rope_w[:, 1, :], rope_w[:, 0, :], ACT.Sin).then_inc(rope_a, 1)
                        act.activation(rope_w[:, 2, :], rope_w[:, 0, :], ACT.Sin, scale=0.5).then_inc(rope_a, 1)
                    empty_piece(("qkv", steps[0].t, k))
                    if k < 4:
                        for kt in (2 * k, 2 * k + 1):
                            empty_norm(layer, kt, 1)
                for what, half in FILLS_BEFORE.values():
                    fill_hi(steps[0].t, what, half)
                for s in steps:
                    before = None if s.first else STEPS[s.t - 1]
                    for slot in range(UNITS):
                        w_hi(SLOT_SPLIT.get((s.t, slot), []))
                        if slot == 2 and before is not None and before.ends_group:
                            silu(before)
                        exps(s, slot)
                        for key in SLOT_PIECES.get((s.t, slot), []):
                            empty_piece(key)
                        b, u = unit_before(s, slot, 1)
                        if b:
                            empty_turn(b, u)
                        if slot in FILLS_WITHIN:
                            fill_hi(s.t, *FILLS_WITHIN[slot])
                        if slot in FILLS_BEFORE and not s.last:
                            fill_hi(s.t + 1, *FILLS_BEFORE[slot])
                        if slot == (1 if layer == 0 else 3) and before is not None and before.ends_group:
                            den_exp(before)
                        if s.last and slot == SPLIT_MIX[0] - 1:
                            silu(s)
                            act.wait_ge(job_done, JOB[("gate", layer, GROUPS - 1)] + 1)
                        if s.last and slot in SPLIT_MIX:
                            k = SPLIT_MIX.index(slot)
                            act.wait_ge(mix_back[k % 3], 16 * (layer * 2 + k // 3 + 1))
                            mix_split(layer, k, mix_in[k % 3])
                last = steps[-1]
                empty_turn(last, UNITS - 1)
                den_exp(last)
                act.wait_ge(mixed, mix_links_before(last.t) + mix_links(last))
                for r in range(2):
                    mix_split(layer, MIX_LOADS + r, ot[out_region(last)][:, r, :])
                for c in range(OUT_JOBS):
                    w_hi(splits_of("job", layer, c))
                    w_hi(splits_of("mid-job", layer, c))
                if layer == 0:
                    norm_half(1, 0)
                    for kt in range(4):
                        empty_norm(1, kt, 0)
                    square(1, 4)
                    square(1, 6)
                    for kt in range(4, KT):
                        empty_norm(1, kt, 0)
                    root(1, 1)
                    scale_rows(1, 1)
                    w_hi(splits_of("next", layer, OUT_JOBS - 1))
            for half in range(2):
                square(2, 4 * half)
                square(2, 4 * half + 2)
                root(2, half)

        @block.vector
        def _(dve):
            def w_lo(quarters):
                for n, q in quarters:
                    if q % 2 == 0:
                        dve.wait_ge(w_hi_done, 4 * n + q + 1)
                        dve.tensor_tensor(quarter(n, q, 1), raw_quarter(n, q), quarter(n, q, 0).bitcast(F32),
                                          ALU.subtract).then_inc(w_lo_done["v"], 1)

            def mask_of(s, n):
                if s.layer == 1 and s.p == 2:
                    return masks[:, 3:4, :]
                if not s.has_prev(n):
                    return masks[:, 2:3, :]
                return masks[:, 1:3, :] if s.layer == 0 else masks[:, 0:3:2, :]

            def mask_max(s, u):
                r, n = u // NB, u % NB
                i = UNITS * s.t + u
                lo = 0 if s.has_prev(n) else P
                dve.wait_ge(scored, i + 1)
                if i >= PROBS:
                    b = i - PROBS
                    dve.wait_ge(turned, TURN.filled((b // UNITS, b % UNITS)))
                if u == 0 and s.layer == 1 and s.t >= GROUPS + 2:
                    dve.wait_ge(stat_out[s.t % 2], stat_stored(s.t - 2))
                for j in range(2):
                    src = s_bank[i % 2][:, 2 * P * j:2 * P * (j + 1)].rearrange("p (e k) -> p e k", e=2)
                    last = dve.tensor_tensor_reduce(probs[:, i % PROBS, j, lo // P:2, :], src[:, lo // P:2, :], mask_of(s, n),
                                                    1.0, -BIG, ALU.add, ALU.max, mx[:, i % 2, j:j + 1])
                last.then_inc(masked, 1)
                dve.wait_ge(masked, i + 1)
                least = neg_sink[:, R * s.g + 2 * r:R * s.g + 2 * r + 2] if s.layer == 0 else no_sink[:, :]
                dve.scalar_tensor_tensor(out=stat[:, s.t % 2, n, 2 * r:2 * r + 2], in0=mx[:, i % 2, :], scalar=-SCALE,
                                         in1=least, op0=ALU.mult, op1=ALU.min).then_inc(biased, 1)

            def empty_piece(key):
                lent = key[0] == "out" and key[2] == 0 and key[3] in SPARE
                if lent:
                    dve.wait_ge(spare_full, len(SPARE) * key[1] + SPARE.index(key[3]) + 1)
                    dve.tensor_tensor(xr[:, key[3], 0:OUT_COLS], spare[key[3]][:, 0:OUT_COLS], res[0][:, key[3], :],
                                      ALU.add).then_inc(spare_empty, 1)
                    return
                if "v" not in PIECE.uses[PIECE.at[key]]:
                    return
                dve.wait_ge(piece_full, PIECE.filled(key))
                src = j_bank[PIECE.bank(key)]
                if key[0] == "qkv":
                    k = key[2]
                    guard_qkv(dve, key)
                    dve.tensor_copy(qk[:, k, 0:R * HD + HD], src[:, 0:R * HD + HD])
                    dve.tensor_copy(qk[:, k, R * HD + HD:], src[:, R * HD:R * HD + HD])
                    last = dve.tensor_copy(v[:, key[1] % 2, k, :], src[:, R * HD + HD:QKV])
                elif key[0] == "gate":
                    r, half = key[3] // 2, key[3] % 2
                    guard_gate(dve, key)
                    last = dve.tensor_copy(gate_of(key[1], key[2])[:, r, half * 512:(half + 1) * 512], src[:, :])
                else:
                    _, layer, c, k = key
                    if k == 0:
                        dve.wait_ge(res_in[c % 2], 16 * (2 * layer + c // 2 + 1))
                    last = dve.tensor_tensor(xr[:, k, c * OUT_COLS:(c + 1) * OUT_COLS], src[:, 0:OUT_COLS],
                                             res[c % 2][:, k, :], ALU.add)
                last.then_inc(piece_empty["v"], 1)

            def empty_norm(layer, kt, half):
                i = KT * half + kt
                cols = slice(half * 512, (half + 1) * 512)
                dve.wait_ge(norm_empty["a"], 2 * KT * layer + i + 1)
                dve.scalar_tensor_tensor(out=ht[1][:, kt, cols], in0=norm_bank[i % 4][:, :],
                                         scalar=gain[:, layer, kt:kt + 1], in1=ht[0][:, kt, cols].bitcast(F32),
                                         op0=ALU.mult, op1=ALU.subtract).then_inc(norm_empty["v"], 1)

            def empty_turn(s, u):
                if u % 2 == 1:
                    store_turn(dve, dve.tensor_copy, s, u).then_inc(turn_empty["v"], 1)

            def fill_lo(t, what, half):
                key = (t, what, half)
                dve.wait_ge(turn_empty["a"], TURN.emptied(key, "a"))
                guard_fill(dve, t, what, half)
                src = t_bank[TURN.bank(key)]
                cols = slice(half * 512, (half + 1) * 512)
                if what == "K":
                    last = dve.tensor_tensor(ks[:, 1, cols], src[:, :], ks[:, 0, cols].bitcast(F32), ALU.subtract)
                else:
                    h = 2 * int(what[1])
                    dve.tensor_tensor(qs[64:P, h, cols], src[0:64, :], qs[0:64, h, cols].bitcast(F32), ALU.subtract)
                    last = dve.tensor_tensor(qs[0:64, h + 1, cols], src[64:P, :], qs[64:P, h + 1, cols].bitcast(F32), ALU.subtract)
                last.then_inc(turn_empty["v"], 1)

            def store_ot(s, r, half):
                group = 4 * s.t + 2 * r + half
                dve.wait_ge(summed, UNITS * s.t + NB * r + 4 * half + 4)
                if s.layer == 1 and r == 0 and half == 0:
                    done = GROUPS - 1 + sum(q.ends_group for q in STEPS[GROUPS:s.t - s.p]) - (s.p == 0 and s.g > 0)
                    dve.wait_ge(mix_out, 32 * done)
                to = patterned(ot[s.t % 4][:, r, :], s.p, half)
                src = o_bank[group % 2][:, :].rearrange("a (b c) -> a b c", b=to.shape[1])
                dve.tensor_copy(to, src).then_inc(ot_stored, 1)

            def link(ins, sem_, value):
                ins.then_inc(sem_, 1)
                dve.wait_ge(sem_, value)

            def coefs_first(s):
                n = links_before(s.t)
                dve.wait_ge(exped, UNITS * (s.t + 1))
                if groups_before(s.t) > 0:
                    before = [q.t for q in STEPS[:s.t] if q.ends_group][-1]
                    dve.wait_ge(turned, TURN.filled(("C", before)))
                if s.layer == 0:
                    sinks = sink[:, R * s.g:R * (s.g + 1)].rearrange("p (o h) -> p o h", o=1).broadcast_to([P, NB, R])
                    link(dve.tensor_tensor(comb[:, 0, 0, :, :], stat[:, s.t % 2, :, 0:R], sinks, ALU.add), den_v, n + 1)
                    return
                dve.wait_ge(nat_in, 48 * (s.g + 1))
                least = comb_small[:, 0, :, :]
                link(dve.tensor_tensor(least, nat[:, 0, :, 0:R], nat[:, 1, :, 0:R], ALU.min), den_v, n + 1)
                link(dve.tensor_tensor(least, least, nat[:, 2, :, 0:R], ALU.min), den_v, n + 2)
                for p in range(3):
                    last = dve.tensor_tensor(comb[:, 0, p, :, :], least, nat[:, p, :, 0:R], ALU.subtract)
                link(last, den_v, n + 3)

            def coefs_last(s):
                n = links_before(s.t)
                dve.wait_ge(den_a, groups_before(s.t) + 1)
                if s.layer == 0:
                    link(dve.tensor_tensor(comb_small[:, 0, :, :], comb[:, 0, 0, :, :], stat[:, s.t % 2, :, R:2 * R], ALU.add), den_v, n + 2)
                    link(dve.reciprocal(comb[:, 1, 0, :, :], comb_small[:, 0, :, :]), den_v, n + 3)
                    dve.sem_inc(den_v, 1)
                    return
                for p in range(3):
                    last = dve.tensor_tensor(comb[:, 1, p, :, :], comb[:, 0, p, :, :], nat[:, p, :, R:2 * R], ALU.mult)
                link(last, den_v, n + 4)
                link(dve.tensor_tensor(comb[:, 1, 0, :, :], comb[:, 1, 0, :, :], comb[:, 1, 1, :, :], ALU.add), den_v, n + 5)
                link(dve.tensor_tensor(comb[:, 1, 0, :, :], comb[:, 1, 0, :, :], comb[:, 1, 2, :, :], ALU.add), den_v, n + 6)
                dve.reciprocal(comb_small[:, 1, :, :], comb[:, 1, 0, :, :]).then_inc(norm_r, 1)
                dve.wait_ge(norm_r, s.g + 1)
                for p in range(3):
                    last = dve.tensor_tensor(comb[:, 0, p, :, :], comb[:, 0, p, :, :], comb_small[:, 1, :, :], ALU.mult)
                link(last, den_v, n + 7)

            def coef_store(s):
                key = ("C", s.t)
                rows = (1 if s.layer == 0 else 3) * NB * R
                dve.wait_ge(turned, TURN.filled(key))
                if groups_before(s.t) > 0:
                    dve.wait_ge(coef_out, 16 * groups_before(s.t))
                dve.tensor_copy(coef_rows[0:rows, :], t_bank[TURN.bank(key)][0:rows, 0:P]).then_inc(turn_empty["v"], 1)

            def mix(s, k):
                items = mix_items(s)
                r, half, p = items[k]
                cols = slice(512 * half, 512 * half + 512)
                index = coef_loads_before(s.t) + k
                done = product_link(index)
                region = out_region(s)
                tile = ot[(region + p) % 4][:, r, cols]
                into = ot[region][:, r, cols]
                dve.wait_ge(coef_in[index % 2], 32 * (index // 2 + 1))
                dve.wait_ge(ot_stored, 4 * (s.t + 1))
                link(dve.tensor_tensor(tile, tile, coef[:, index % 2, :], ALU.mult), mixed, done)
                if p > 0:
                    done += 1
                    link(dve.tensor_tensor(into, into, tile, ALU.add), mixed, done)
                if k + 1 == len(items) or items[k + 1][2] == 0:
                    dve.wait_ge(silued, groups_before(s.t) + 1)
                    link(dve.tensor_tensor(into, into, gate_of(s.layer, s.g)[:, r, cols], ALU.mult), mixed, done + 1)

            def mix_split(layer, k, src):
                dve.wait_ge(mix_hi, layer * (MIX_LOADS + 2) + k + 1)
                dve.tensor_tensor(ht[1][:, k, :], src, ht[0][:, k, :].bitcast(F32), ALU.subtract).then_inc(mix_lo, 1)

            def square(k, n):
                row_ready(k)(dve, n)
                count = 4 * k + n // 2
                if count > 0:
                    dve.wait_ge(squared["v"], count)
                dve.tensor_tensor_reduce(square_v, xr[:, n, :], xr[:, n, :], 1.0, 0.0, ALU.mult, ALU.add,
                                         sums[:, n:n + 1]).then_inc(squared["v"], 1)

            def inverse_rms(k, half):
                base = NORM_LINKS * (2 * k + half)
                blocks = slice(4 * half, 4 * half + 4)
                var, y, z = ssq[:, 0, blocks], ssq[:, 2, blocks], ssq[:, 3, blocks]
                dve.wait_ge(squared["a"], 4 * k + 2 * half + 2)
                dve.wait_ge(squared["v"], 4 * k + 2 * half + 2)
                link(dve.tensor_scalar(var, sums[:, blocks], 1.0 / D, EPS, ALU.mult, ALU.add), norm_v, base + 1)
                dve.wait_ge(norm_a, 2 * k + half + 1)
                link(dve.reciprocal(y, ssq[:, 1, blocks]), norm_v, base + 2)
                link(dve.tensor_tensor(z, y, y, ALU.mult), norm_v, base + 3)
                link(dve.tensor_tensor(z, z, var, ALU.mult), norm_v, base + 4)
                link(dve.tensor_scalar(z, z, -0.5, 1.5, ALU.mult, ALU.add), norm_v, base + 5)
                link(dve.tensor_tensor(y, y, z, ALU.mult), norm_v, base + 6)

            def scale_rows(layer, half):
                guard_scale(dve, layer, half)
                for n in (4 * half + 1, 4 * half + 3):
                    dve.tensor_scalar(xr[:, n, :], xr[:, n, :], ssq[:, 2, n:n + 1], None, ALU.mult).then_inc(xn_done["v"], 1)

            def norm_half(layer, half):
                square(layer, 4 * half + 1)
                square(layer, 4 * half + 3)
                inverse_rms(layer, half)
                scale_rows(layer, half)

            def final_rows(blocks):
                for n in blocks:
                    dve.scalar_tensor_tensor(out=xr[:, n, :], in0=xr[:, n, :], scalar=ssq[:, 2, n:n + 1], in1=gain_row,
                                             op0=ALU.mult, op1=ALU.mult).then_inc(final_done, 1)

            def constants():
                dve.tensor_scalar(neg_sink[:, :], sink[:, :], -1.0, None, ALU.mult).then_inc(sink_neg, 1)
                dve.wait_ge(sink_neg, 1)
                dve.wait_ge(consts, 1)
                odd = gate[:, 1, P:2 * P]
                link(dve.tensor_scalar(parity[:, :], parity[:, :], 1, None, ALU.bitwise_and), mask_v, 1)
                link(dve.tensor_scalar(odd, parity[:, :], MASKED, None, ALU.mult), mask_v, 2)
                link(dve.tensor_tensor(masks[:, 3, :], masks[:, 3, :], odd, ALU.add), mask_v, 3)

            def rope_tables():
                n = [0]

                def chain(ins):
                    n[0] += 1
                    link(ins, rope_v, n[0])

                ang = rope_w[:, 0, :].rearrange("p (t j) -> p t j", j=HALF_ROT)
                turns = rope_w[:, 1, :]
                part = rope_w[:, 2, :]
                chain(dve.tensor_copy(pos_f[:, :, :], pos_i[:, :, :]))
                flat = pos_f[:, :, :].rearrange("p a b -> p (a b)")
                for j in range(HALF_ROT):
                    freq = float(np.float32(THETA ** (-j / HALF_ROT)))
                    last = dve.tensor_scalar(ang[:, :, j], flat, freq, None, ALU.mult)
                chain(last)
                magic = 1.5 * 2.0 ** 23
                for period in (2 * np.pi * 256, 2 * np.pi):
                    rest, parts = period, []
                    for bits in (9, 9):
                        unit = 2.0 ** (np.floor(np.log2(rest)) - bits + 1)
                        parts.append(np.floor(rest / unit) * unit)
                        rest -= parts[-1]
                    parts.append(rest)
                    chain(dve.tensor_scalar(turns, rope_w[:, 0, :], float(1.0 / period), magic, ALU.mult, ALU.add))
                    chain(dve.tensor_scalar(turns, turns, -magic, None, ALU.add))
                    for c in parts:
                        chain(dve.tensor_scalar(part, turns, float(c), None, ALU.mult))
                        chain(dve.tensor_tensor(rope_w[:, 0, :], rope_w[:, 0, :], part, ALU.subtract))
                for _ in range(ROPE_LINKS - 2 - 16 - 1):
                    dve.sem_inc(rope_v, 1)
                    n[0] += 1
                pi = float(np.nextafter(np.float32(np.pi), np.float32(0)))
                chain(dve.tensor_scalar(rope_w[:, 0, :], rope_w[:, 0, :], pi, -pi, ALU.min, ALU.max))
                dve.wait_ge(rope_a, 2)
                sin = rope_w[:, 1, :].rearrange("p (t j) -> p t j", j=HALF_ROT)
                half = rope_w[:, 2, :]
                cos_to = cosines[:, :, :, :].rearrange("p a b c -> p (a b) c")
                sin_to = sines[:, :, :, :].rearrange("p a b c -> p (a b) c")
                dve.tensor_copy(sin_to[:, :, HALF_ROT:ROT], sin)
                dve.tensor_scalar(sin_to[:, :, 0:HALF_ROT], sin, -1.0, None, ALU.mult)
                chain(dve.tensor_tensor(half, half, half, ALU.mult))
                halves = half.rearrange("p (t j) -> p t j", j=HALF_ROT)
                dve.tensor_scalar(cos_to[:, :, 0:HALF_ROT], halves, -2.0, 1.0, ALU.mult, ALU.add)
                chain(dve.tensor_scalar(cos_to[:, :, HALF_ROT:ROT], halves, -2.0, 1.0, ALU.mult, ALU.add))
                dve.sem_inc(tables, 1)

            norm_half(0, 0)
            w_lo(splits_of("start"))
            dve.wait_ge(small_in, 16 * 3)
            for kt in range(KT):
                empty_norm(0, kt, 0)
            norm_half(0, 1)
            w_lo(splits_of("start, later"))
            for layer in (0, 1):
                steps = LAYER_STEPS[layer]
                for k in range(NB):
                    if layer == 0 and k == 3:
                        rope_tables()
                        constants()
                    empty_piece(("qkv", steps[0].t, k))
                    if k < 4:
                        for kt in (2 * k, 2 * k + 1):
                            empty_norm(layer, kt, 1)
                for what, half in FILLS_BEFORE.values():
                    fill_lo(steps[0].t, what, half)
                for s in steps:
                    before = None if s.first else STEPS[s.t - 1]
                    for slot in range(UNITS):
                        mask_max(s, slot)
                        w_lo(SLOT_SPLIT.get((s.t, slot), []))
                        for key in SLOT_PIECES.get((s.t, slot), []):
                            empty_piece(key)
                        b, u = unit_before(s, slot, 1)
                        if b:
                            empty_turn(b, u)
                        if slot in FILLS_WITHIN:
                            fill_lo(s.t, *FILLS_WITHIN[slot])
                        if slot in FILLS_BEFORE and not s.last:
                            fill_lo(s.t + 1, *FILLS_BEFORE[slot])
                        if before is not None and before.ends_group:
                            if slot == (1 if layer == 0 else 3):
                                coefs_first(before)
                            if slot == (2 if layer == 0 else 4):
                                coefs_last(before)
                            if slot == LATE_C:
                                coef_store(before)
                            for k in range(len(mix_items(before))):
                                if mix_slot(before, k) == slot:
                                    mix(before, k)
                        if s.last and slot in SPLIT_MIX:
                            k = SPLIT_MIX.index(slot)
                            mix_split(layer, k, mix_in[k % 3])
                        b, u = unit_before(s, slot, 2)
                        if b and u % 4 == 3:
                            store_ot(b, u // NB, (u % NB) // 4)
                last = steps[-1]
                empty_turn(last, UNITS - 1)
                if layer == 0:
                    coefs_first(last)
                    coefs_last(last)
                store_ot(last, 1, 1)
                if layer == 1:
                    coefs_first(last)
                    coefs_last(last)
                coef_store(last)
                for k in range(len(mix_items(last))):
                    mix(last, k)
                for r in range(2):
                    mix_split(layer, MIX_LOADS + r, ot[out_region(last)][:, r, :])
                for c in range(OUT_JOBS):
                    w_lo(splits_of("job", layer, c))
                    for k in range(NB):
                        empty_piece(("out", layer, c, k))
                        if k == 2:
                            w_lo(splits_of("mid-job", layer, c))
                        if c < OUT_JOBS - 1:
                            continue
                        if k % 2 == 1:
                            square(layer + 1, k)
                        if k == 4:
                            inverse_rms(layer + 1, 0)
                            if layer == 0:
                                scale_rows(1, 0)
                            else:
                                dve.wait_ge(gain_in, 16)
                                final_rows(range(0, 1))
                        if layer == 1 and k in (5, 6):
                            final_rows(range(2 * k - 9, 2 * k - 9 + (2 if k == 5 else 1)))
                        if layer == 0 and k >= 6:
                            for kt in range(4 * (k - 6), 4 * (k - 6) + 4):
                                empty_norm(1, kt, 0)
                inverse_rms(layer + 1, 1)
                if layer == 0:
                    scale_rows(1, 1)
                    w_lo(splits_of("next", layer, OUT_JOBS - 1))
                else:
                    final_rows(range(4, NB))


def by_block(a, p):
    if p == 0:
        return a.reshape(NB, P).T
    if p == 1:
        return a.reshape(2, P, 4).transpose(1, 2, 0).reshape(P, NB)
    return a.reshape(P, NB)


def by_partition(w):
    return w.reshape(KT, P, w.shape[1]).transpose(1, 0, 2).reshape(P, -1)


def kernel(**inputs):
    import concourse.bacc as bacc
    from concourse.bass_utils import run_bass_kernel_spmd

    a = {name: np.asarray(value) for name, value in inputs.items()}
    w_in = [a["w_in_0"], a["w_in_1"]]
    qkv = []
    for s in STEPS:
        base, w = s.p * PER, w_in[s.layer]
        q0, k0, v0 = base + s.g * R * HD, base + D + s.g * HD, base + D + KV + s.g * HD
        qkv.append(by_partition(np.concatenate([w[:, q0:q0 + R * HD], w[:, k0:k0 + HD], w[:, v0:v0 + HD]], axis=1)))
    gates = [w_in[layer][:, base + g * R * HD:base + (g + 1) * R * HD]
             for layer, base in ((0, PER), (1, 3 * PER)) for g in range(GROUPS)]
    outs = [a[name][:, c * OUT_COLS:(c + 1) * OUT_COLS] for name in ("w_out_0", "w_out_1") for c in range(OUT_JOBS)]
    arrays = {
        "x": a["x"],
        "positions": np.stack([by_block(a["positions"][0], p) for p in range(3)], axis=1),
        "gains": np.stack([a[name].reshape(KT, P).T for name in ("norm_0", "norm_1")], axis=1),
        "sinks_0": a["sinks_0"],
        "final_norm": a["final_norm"],
        "w_qkv": np.stack(qkv),
        "w_gate": np.stack([by_partition(w) for w in gates]),
        "w_out": np.stack([by_partition(w) for w in outs]),
    }
    arrays = {f"in_{name}": np.ascontiguousarray(value) for name, value in arrays.items()}
    nc = bacc.Bacc("TRN2", target_bir_lowering=False, num_devices=1)
    args = [nc.dram_tensor(name, value.shape, mybir.dt.from_np(value.dtype), kind="ExternalInput").ap()
            for name, value in arrays.items()]
    args.append(nc.dram_tensor("out_0", (1, S, D), F32, kind="ExternalOutput").ap())
    trunk(nc, *args)
    got = run_bass_kernel_spmd(nc, [arrays], core_ids=[0])
    return got.results[0]["out_0"]
```
